# Optimizing a Trainium2 kernel written in Bass

```python
import jax, jax.numpy as jnp
from jax import lax
import numpy as np

D_MODEL = 1024
BATCH = 1
SEQ = 256
DEPTH = 1

N_MEM = 256
A_HEADS = 8
A_HEAD_DIM = 64
A_WIDTH = A_HEADS * A_HEAD_DIM
IDX_HEADS = 8
IDX_DIM = 64
TOPK_MAX = 256
Q_BLOCK = 128
CONV_WIDTH = 512
CONV_K = 3
X_HEADS = 4
X_HEAD_DIM = D_MODEL // X_HEADS
D_FF = 2816
ROPE_THETA = 10000.0
EPS = 1e-6

SPLITS = (A_WIDTH, A_HEAD_DIM, A_HEAD_DIM, IDX_HEADS * IDX_DIM, IDX_DIM, IDX_HEADS,
          CONV_WIDTH, CONV_WIDTH, CONV_WIDTH, D_MODEL, D_MODEL)
IN_WIDTH = (A_WIDTH + 2 * A_HEAD_DIM + IDX_HEADS * IDX_DIM + IDX_DIM + IDX_HEADS
            + 3 * CONV_WIDTH + 2 * D_MODEL)


def rms_norm(x, g):
    xf = x.astype(jnp.float32)
    y = xf * lax.rsqrt(jnp.mean(xf * xf, axis=-1, keepdims=True) + EPS)
    return (y * g.astype(jnp.float32)).astype(x.dtype)

def rope_tables(seq_len, dim):
    pos = jnp.arange(seq_len, dtype=jnp.float32)
    inv = ROPE_THETA ** (-jnp.arange(0, dim, 2, dtype=jnp.float32) / dim)
    ang = pos[:, None] * inv[None, :]
    return jnp.cos(ang), jnp.sin(ang)

def apply_rope(x, cos, sin):
    xf = x.astype(jnp.float32)
    half = xf.shape[-1] // 2
    x1, x2 = xf[..., :half], xf[..., half:]
    c = cos[None, :, None, :]
    s = sin[None, :, None, :]
    return jnp.concatenate([x1 * c - x2 * s, x2 * c + x1 * s], axis=-1).astype(x.dtype)

def swiglu(x, w1, w3, w2):
    return (jax.nn.silu(x @ w1) * (x @ w3)) @ w2

def dsa_attention(q, k, v, q_idx, k_idx, w_idx):
    b, seq_len, n_heads, head_dim = q.shape
    k_top = min(TOPK_MAX, seq_len // 4)
    n_blocks = seq_len // Q_BLOCK
    key_pos = jnp.arange(seq_len)
    idx_scale = IDX_DIM ** -0.5
    attn_scale = head_dim ** -0.5

    def to_blocks(a):
        return a.reshape((b, n_blocks, Q_BLOCK) + a.shape[2:]).swapaxes(0, 1)

    def block(args):
        qb, qib, wb, t0 = args
        qpos = t0 + jnp.arange(Q_BLOCK)
        raw = jnp.einsum('bqhd,bsd->bqhs', qib, k_idx).astype(jnp.float32) * idx_scale
        score = jnp.einsum('bqhs,bqh->bqs', jax.nn.relu(raw), wb.astype(jnp.float32))
        causal = key_pos[None, :] <= qpos[:, None]
        score = jnp.where(causal[None], score, -jnp.inf)
        _, sel = lax.top_k(score, k_top)
        k_sel = jax.vmap(lambda kb, ib: kb[ib])(k, sel)
        v_sel = jax.vmap(lambda vb, ib: vb[ib])(v, sel)
        logits = jnp.einsum('bqhd,bqkd->bqhk', qb, k_sel).astype(jnp.float32) * attn_scale
        valid = (sel <= qpos[None, :, None])[:, :, None, :]
        logits = jnp.where(valid, logits, -jnp.inf)
        p = jax.nn.softmax(logits, axis=-1)
        return jnp.einsum('bqhk,bqkd->bqhd', p.astype(v.dtype), v_sel)

    outs = lax.map(block, (to_blocks(q), to_blocks(q_idx), to_blocks(w_idx),
                           jnp.arange(n_blocks) * Q_BLOCK))
    return outs.swapaxes(0, 1).reshape(b, seq_len, n_heads * head_dim)

def short_conv_causal(z, conv_w):
    c = z.shape[-1]
    kern = conv_w.reshape(CONV_K, 1, c).astype(z.dtype)
    return lax.conv_general_dilated(z, kern, window_strides=(1,), padding=[(CONV_K - 1, 0)],
                                    dimension_numbers=('NWC', 'WIO', 'NWC'),
                                    feature_group_count=c)

def memory_cross_attention(h, mem_n, w_q, w_kv, w_o):
    b, s, _ = h.shape
    m = mem_n.shape[1]
    q = (h @ w_q).reshape(b, s, X_HEADS, X_HEAD_DIM)
    kv = (mem_n @ w_kv).reshape(b, m, 2, X_HEADS, X_HEAD_DIM)
    k, v = kv[:, :, 0], kv[:, :, 1]
    logits = jnp.einsum('bshd,bmhd->bhsm', q, k).astype(jnp.float32) * (X_HEAD_DIM ** -0.5)
    p = jax.nn.softmax(logits, axis=-1)
    o = jnp.einsum('bhsm,bmhd->bshd', p.astype(v.dtype), v)
    return o.reshape(b, s, D_MODEL) @ w_o

def first_inputs(seed: int = 0) -> dict:
    key = jax.random.key(seed)
    ks = iter(jax.random.split(key, 32))

    def w(shape, fan_in):
        return jax.random.normal(next(ks), (DEPTH,) + shape, jnp.float32) * fan_in ** -0.5

    def gain(n):
        return 1.0 + 0.05 * jax.random.normal(next(ks), (DEPTH, n), jnp.float32)

    x = jax.random.normal(next(ks), (BATCH, SEQ, D_MODEL), jnp.float32)
    mem = jax.random.normal(next(ks), (BATCH, N_MEM, D_MODEL), jnp.float32)
    return {
        "x": x,
        "mem": mem,
        "ffn1_pre_g": gain(D_MODEL),
        "ffn1_post_g": gain(D_MODEL),
        "ffn1_w1": w((D_MODEL, D_FF), D_MODEL),
        "ffn1_w3": w((D_MODEL, D_FF), D_MODEL),
        "ffn1_w2": w((D_FF, D_MODEL), D_FF),
        "mix_pre_g": gain(D_MODEL),
        "mix_post_g": gain(D_MODEL),
        "w_in": w((D_MODEL, IN_WIDTH), D_MODEL),
        "conv_w": w((CONV_K, CONV_WIDTH), CONV_K),
        "w_a_out": w((A_WIDTH, D_MODEL), A_WIDTH),
        "w_b_out": w((CONV_WIDTH, D_MODEL), CONV_WIDTH),
        "w_out": w((D_MODEL, D_MODEL), D_MODEL),
        "mem_g": gain(D_MODEL),
        "xattn_pre_g": gain(D_MODEL),
        "xattn_post_g": gain(D_MODEL),
        "xattn_w_q": w((D_MODEL, D_MODEL), D_MODEL),
        "xattn_w_kv": w((D_MODEL, 2 * D_MODEL), D_MODEL),
        "xattn_w_o": w((D_MODEL, D_MODEL), D_MODEL),
        "ffn2_pre_g": gain(D_MODEL),
        "ffn2_post_g": gain(D_MODEL),
        "ffn2_w1": w((D_MODEL, D_FF), D_MODEL),
        "ffn2_w3": w((D_MODEL, D_FF), D_MODEL),
        "ffn2_w2": w((D_FF, D_MODEL), D_FF),
    }

def first_block(x, mem, ffn1_pre_g, ffn1_post_g, ffn1_w1, ffn1_w3, ffn1_w2,
              mix_pre_g, mix_post_g, w_in, conv_w, w_a_out, w_b_out, w_out,
              mem_g, xattn_pre_g, xattn_post_g, xattn_w_q, xattn_w_kv, xattn_w_o,
              ffn2_pre_g, ffn2_post_g, ffn2_w1, ffn2_w3, ffn2_w2):
    b, seq_len, _ = x.shape
    cos_a, sin_a = rope_tables(seq_len, A_HEAD_DIM)
    cos_i, sin_i = rope_tables(seq_len, IDX_DIM)
    split_points = np.cumsum(np.array(SPLITS))[:-1].tolist()
    h = x
    for l in range(DEPTH):
        f = swiglu(rms_norm(h, ffn1_pre_g[l]), ffn1_w1[l], ffn1_w3[l], ffn1_w2[l])
        h = h + 0.5 * rms_norm(f, ffn1_post_g[l])

        u = rms_norm(h, mix_pre_g[l])
        proj = u @ w_in[l]
        (q_a, k_a, v_a, q_i, k_i, w_i, gate_b, gate_c, conv_in,
         g_a, g_b) = jnp.split(proj, split_points, axis=-1)

        q_a = apply_rope(q_a.reshape(b, seq_len, A_HEADS, A_HEAD_DIM), cos_a, sin_a)
        k_a = apply_rope(k_a[:, :, None, :], cos_a, sin_a)[:, :, 0]
        q_i = apply_rope(q_i.reshape(b, seq_len, IDX_HEADS, IDX_DIM), cos_i, sin_i)
        k_i = apply_rope(k_i[:, :, None, :], cos_i, sin_i)[:, :, 0]
        w_i = w_i * (IDX_HEADS ** -0.5)
        y_a = dsa_attention(q_a, k_a, v_a, q_i, k_i, w_i) @ w_a_out[l]

        z = short_conv_causal(gate_c * conv_in, conv_w[l])
        y_b = (gate_b * z) @ w_b_out[l]

        merged = jax.nn.sigmoid(g_a) * y_a + jax.nn.sigmoid(g_b) * y_b
        h = h + rms_norm(merged @ w_out[l], mix_post_g[l])

        c = memory_cross_attention(rms_norm(h, xattn_pre_g[l]), rms_norm(mem, mem_g[l]),
                                   xattn_w_q[l], xattn_w_kv[l], xattn_w_o[l])
        h = h + rms_norm(c, xattn_post_g[l])

        f = swiglu(rms_norm(h, ffn2_pre_g[l]), ffn2_w1[l], ffn2_w3[l], ffn2_w2[l])
        h = h + 0.5 * rms_norm(f, ffn2_post_g[l])
    return h


DEPTH_2 = 2

N_A_LAYERS = DEPTH_2 // 2
N_B_LAYERS = DEPTH_2 - N_A_LAYERS
HEAD_DIM = 64
RWKV_HEADS = D_MODEL // HEAD_DIM
D_DECAY_LORA = max(32, int(round(1.8 * D_MODEL ** 0.5 / 32)) * 32)
D_AAA_LORA = max(32, int(round(1.8 * D_MODEL ** 0.5 / 32)) * 32)
D_MV_LORA = max(32, int(round(1.3 * D_MODEL ** 0.5 / 32)) * 32)
D_GATE_LORA = max(32, int(round(0.6 * D_MODEL ** 0.8 / 32)) * 32)
GN_EPS = 64e-5
N_Q_HEADS = D_MODEL // HEAD_DIM
N_KV_HEADS = 2
GROUP = N_Q_HEADS // N_KV_HEADS
WINDOW = 128
BLOCK = WINDOW
FFN_DIM = 4 * D_MODEL
RMS_EPS = 1e-6


def rms_norm_2(x, g):
    xf = x.astype(jnp.float32)
    y = xf * lax.rsqrt(jnp.mean(xf * xf, axis=-1, keepdims=True) + RMS_EPS)
    return (y * g.astype(jnp.float32)).astype(x.dtype)

def squared_relu_mlp(h, w1, w2):
    return jnp.square(jax.nn.relu(h @ w1)) @ w2

def token_shift(x):
    return jnp.pad(x, ((0, 0), (1, 0), (0, 0)))[:, :-1]

def wkv7(r, w, k, v, a, b):
    B, T, H, N = r.shape
    s0 = jnp.zeros((B, H, N, N), jnp.float32)

    def step(S, inp):
        r_t, w_t, k_t, v_t, a_t, b_t = inp
        sa = jnp.einsum('bhvk,bhk->bhv', S, a_t)
        S = S * w_t[:, :, None, :] + sa[..., None] * b_t[:, :, None, :] + v_t[..., None] * k_t[:, :, None, :]
        y = jnp.einsum('bhvk,bhk->bhv', S, r_t)
        return S, y

    xs = tuple(jnp.moveaxis(t, 1, 0) for t in (r, w, k, v, a, b))
    _, ys = lax.scan(step, s0, xs)
    return jnp.moveaxis(ys, 0, 1)

def rwkv7_time_mix(h, v_first, vres, mu, w_rkv, w0, w1, w2, a0, a1, a2, g1, g2, k_k, k_a, r_k, gn_g, gn_b, wo):
    f32 = jnp.float32
    B, T, C = h.shape
    H, N = RWKV_HEADS, HEAD_DIM
    xx = token_shift(h) - h
    xs = h[None] + xx[None] * mu[:, None, None, :]
    r, k, v = jnp.einsum('nbtc,ncd->nbtd', xs[:3], w_rkv)
    xv, xw, xa, xg = xs[2], xs[3], xs[4], xs[5]
    w_log = -jax.nn.softplus(-(w0 + jnp.tanh(xw @ w1) @ w2).astype(f32)) - 0.5
    decay = jnp.exp(-jnp.exp(w_log))
    if vres is None:
        v_first = v
    else:
        v0, v1, v2 = vres
        v = v + (v_first - v) * jax.nn.sigmoid(v0 + (xv @ v1) @ v2)
    a = jax.nn.sigmoid(a0 + (xa @ a1) @ a2)
    g = jax.nn.sigmoid(xg @ g1) @ g2

    def split(t):
        return t.reshape(B, T, H, N).astype(f32)

    kk = split(k * k_k)
    kk = kk / jnp.maximum(jnp.sqrt(jnp.sum(kk * kk, axis=-1, keepdims=True)), 1e-12)
    k_mod = k * (1.0 + (a - 1.0) * k_a)
    rh, kh, vh, ah, wh = split(r), split(k_mod), split(v), split(a), split(decay)
    y = wkv7(rh, wh, kh, vh, -kk, kk * ah)
    mean = jnp.mean(y, axis=-1, keepdims=True)
    var = jnp.mean(jnp.square(y - mean), axis=-1, keepdims=True)
    y = (y - mean) * lax.rsqrt(var + GN_EPS) * gn_g.reshape(H, N).astype(f32) + gn_b.reshape(H, N).astype(f32)
    y = y + jnp.sum(rh * kh * r_k.astype(f32), axis=-1, keepdims=True) * vh
    out = (y.reshape(B, T, C).astype(h.dtype) * g) @ wo
    return out, v_first

def shared_kv(x, kv_norm, w_kv, k_gain):
    B, T, _ = x.shape
    kv = (rms_norm_2(x, kv_norm) @ w_kv).reshape(B, T, 2, N_KV_HEADS, HEAD_DIM)
    k = rms_norm_2(kv[:, :, 0], k_gain)
    v = kv[:, :, 1]
    return k, v

def swa_sink_attention(q, k, v, sinks):
    B, T, _, D = q.shape
    nb = T // BLOCK
    qb = q.reshape(B, nb, BLOCK, N_KV_HEADS, GROUP, D)
    kb = k.reshape(B, nb, BLOCK, N_KV_HEADS, D)
    vb = v.reshape(B, nb, BLOCK, N_KV_HEADS, D)
    pad = ((0, 0), (1, 0), (0, 0), (0, 0), (0, 0))
    kcat = jnp.concatenate([jnp.pad(kb, pad)[:, :-1], kb], axis=2)
    vcat = jnp.concatenate([jnp.pad(vb, pad)[:, :-1], vb], axis=2)
    s = jnp.einsum('bnqhgd,bnshd->bnhgqs', qb, kcat, preferred_element_type=jnp.float32)
    qi = jnp.arange(BLOCK)[:, None]
    kj = jnp.arange(2 * BLOCK)[None, :]
    dist = qi + BLOCK - kj
    blk = jnp.arange(nb)[:, None, None]
    valid = (dist >= 0)[None] & (dist < WINDOW)[None] & ((blk > 0) | (kj >= BLOCK)[None])
    slopes = jnp.exp2(-8.0 * jnp.arange(1, N_Q_HEADS + 1, dtype=jnp.float32) / N_Q_HEADS)
    alibi = slopes.reshape(N_KV_HEADS, GROUP)[:, :, None, None] * dist.astype(jnp.float32)
    s = jnp.where(valid[None, :, None, None], s - alibi, -jnp.inf)
    sink = sinks.astype(jnp.float32).reshape(N_KV_HEADS, GROUP)[None, None, :, :, None, None]
    m = jnp.maximum(jnp.max(s, axis=-1, keepdims=True), sink)
    p = jnp.exp(s - m)
    p = p / (jnp.sum(p, axis=-1, keepdims=True) + jnp.exp(sink - m))
    o = jnp.einsum('bnhgqs,bnshd->bnqhgd', p.astype(v.dtype), vcat)
    return o.reshape(B, T, N_Q_HEADS * D)

def swa_layer(h, k_sh, v_sh, wq, q_gain, sinks, wo):
    B, T, _ = h.shape
    q = (h @ wq).reshape(B, T, N_Q_HEADS, HEAD_DIM)
    q = rms_norm_2(q, q_gain) * (HEAD_DIM ** -0.5)
    return swa_sink_attention(q, k_sh, v_sh, sinks) @ wo

def second_inputs(seed: int = 0) -> dict:
    key = jax.random.key(seed)
    ks = iter(jax.random.split(key, 40))
    f32 = jnp.float32
    C, F, NA, NB = D_MODEL, FFN_DIM, N_A_LAYERS, N_B_LAYERS

    def nrm(shape, scale):
        return jax.random.normal(next(ks), shape, f32) * scale

    def gain(shape):
        return 1.0 + nrm(shape, 0.02)

    return {
        'x': nrm((BATCH, SEQ, C), 1.0),
        'ln_mix': gain((DEPTH_2, C)),
        'ln_mlp': gain((DEPTH_2, C)),
        'mlp_w1': nrm((DEPTH_2, C, F), C ** -0.5),
        'mlp_w2': nrm((DEPTH_2, F, C), F ** -0.5),
        'a_mu': jax.random.uniform(next(ks), (NA, 6, C), f32),
        'a_w_rkv': nrm((NA, 3, C, C), C ** -0.5),
        'a_w0': jax.random.uniform(next(ks), (NA, C), f32, -6.0, -0.5),
        'a_w1': nrm((NA, C, D_DECAY_LORA), C ** -0.5),
        'a_w2': nrm((NA, D_DECAY_LORA, C), 0.1 * D_DECAY_LORA ** -0.5),
        'a_a0': nrm((NA, C), 0.5),
        'a_a1': nrm((NA, C, D_AAA_LORA), C ** -0.5),
        'a_a2': nrm((NA, D_AAA_LORA, C), 0.1 * D_AAA_LORA ** -0.5),
        'a_g1': nrm((NA, C, D_GATE_LORA), C ** -0.5),
        'a_g2': nrm((NA, D_GATE_LORA, C), D_GATE_LORA ** -0.5),
        'a_k_k': 0.85 + nrm((NA, C), 0.05),
        'a_k_a': 1.0 + nrm((NA, C), 0.05),
        'a_r_k': nrm((NA, RWKV_HEADS, HEAD_DIM), 0.1),
        'a_gn_g': gain((NA, C)),
        'a_gn_b': nrm((NA, C), 0.02),
        'a_wo': nrm((NA, C, C), C ** -0.5),
        'a_v0': 1.0 + nrm((NA - 1, C), 0.1),
        'a_v1': nrm((NA - 1, C, D_MV_LORA), C ** -0.5),
        'a_v2': nrm((NA - 1, D_MV_LORA, C), 0.1 * D_MV_LORA ** -0.5),
        'kv_norm': gain((C,)),
        'w_kv': nrm((C, 2 * N_KV_HEADS * HEAD_DIM), C ** -0.5),
        'k_gain': gain((HEAD_DIM,)),
        'b_wq': nrm((NB, C, N_Q_HEADS * HEAD_DIM), C ** -0.5),
        'b_q_gain': gain((NB, HEAD_DIM)),
        'b_sinks': nrm((NB, N_Q_HEADS), 0.5),
        'b_wo': nrm((NB, N_Q_HEADS * HEAD_DIM, C), (N_Q_HEADS * HEAD_DIM) ** -0.5),
    }

def second_block(x, ln_mix, ln_mlp, mlp_w1, mlp_w2, a_mu, a_w_rkv, a_w0, a_w1, a_w2, a_a0, a_a1, a_a2, a_g1, a_g2, a_k_k, a_k_a, a_r_k, a_gn_g, a_gn_b, a_wo, a_v0, a_v1, a_v2, kv_norm, w_kv, k_gain, b_wq, b_q_gain, b_sinks, b_wo):
    v_first = None
    k_sh = None
    v_sh = None
    for i in range(DEPTH_2):
        h = rms_norm_2(x, ln_mix[i])
        if i < N_A_LAYERS:
            j = i
            vres = None if j == 0 else (a_v0[j - 1], a_v1[j - 1], a_v2[j - 1])
            out, v_first = rwkv7_time_mix(h, v_first, vres, a_mu[j], a_w_rkv[j], a_w0[j], a_w1[j], a_w2[j], a_a0[j], a_a1[j], a_a2[j], a_g1[j], a_g2[j], a_k_k[j], a_k_a[j], a_r_k[j], a_gn_g[j], a_gn_b[j], a_wo[j])
        else:
            j = i - N_A_LAYERS
            out = swa_layer(h, k_sh, v_sh, b_wq[j], b_q_gain[j], b_sinks[j], b_wo[j])
        x = x + out
        x = x + squared_relu_mlp(rms_norm_2(x, ln_mlp[i]), mlp_w1[i], mlp_w2[i])
        if i == N_A_LAYERS - 1:
            k_sh, v_sh = shared_kv(x, kv_norm, w_kv, k_gain)
    return x


def setup_inputs(seed=0):
    out = dict(first_inputs(seed))
    for name, value in second_inputs(seed + 1).items():
        if name != "x":
            out[name + "_2"] = value
    return out


def reference(
    x, mem, ffn1_pre_g, ffn1_post_g, ffn1_w1, ffn1_w3, ffn1_w2, mix_pre_g, mix_post_g, w_in,
    conv_w, w_a_out, w_b_out, w_out, mem_g, xattn_pre_g, xattn_post_g, xattn_w_q, xattn_w_kv,
    xattn_w_o, ffn2_pre_g, ffn2_post_g, ffn2_w1, ffn2_w3, ffn2_w2, ln_mix_2, ln_mlp_2, mlp_w1_2,
    mlp_w2_2, a_mu_2, a_w_rkv_2, a_w0_2, a_w1_2, a_w2_2, a_a0_2, a_a1_2, a_a2_2, a_g1_2, a_g2_2,
    a_k_k_2, a_k_a_2, a_r_k_2, a_gn_g_2, a_gn_b_2, a_wo_2, a_v0_2, a_v1_2, a_v2_2, kv_norm_2,
    w_kv_2, k_gain_2, b_wq_2, b_q_gain_2, b_sinks_2, b_wo_2,
):
    x = first_block(
        x, mem, ffn1_pre_g, ffn1_post_g, ffn1_w1, ffn1_w3, ffn1_w2, mix_pre_g, mix_post_g, w_in,
        conv_w, w_a_out, w_b_out, w_out, mem_g, xattn_pre_g, xattn_post_g, xattn_w_q,
        xattn_w_kv, xattn_w_o, ffn2_pre_g, ffn2_post_g, ffn2_w1, ffn2_w3, ffn2_w2,
    )
    return second_block(
        x, ln_mix_2, ln_mlp_2, mlp_w1_2, mlp_w2_2, a_mu_2, a_w_rkv_2, a_w0_2, a_w1_2, a_w2_2,
        a_a0_2, a_a1_2, a_a2_2, a_g1_2, a_g2_2, a_k_k_2, a_k_a_2, a_r_k_2, a_gn_g_2, a_gn_b_2,
        a_wo_2, a_v0_2, a_v1_2, a_v2_2, kv_norm_2, w_kv_2, k_gain_2, b_wq_2, b_q_gain_2,
        b_sinks_2, b_wo_2,
    )


_drawn_inputs = setup_inputs


def setup_inputs(seed=0):
    import zlib

    import numpy as np

    out = dict(_drawn_inputs(seed))
    spreads = {}
    factors = {'ffn2_post_g': 3.524,
     'ln_mix_2': 4.888,
     'ln_mlp_2': 3.497,
     'a_w1_2': 8.0,
     'a_w2_2': 8.0,
     'a_a1_2': 4.767,
     'a_a2_2': 4.774,
     'a_gn_g_2': 30.122,
     'a_gn_b_2': 31.937,
     'kv_norm_2': 8.0,
     'k_gain_2': 8.0,
     'b_q_gain_2': 8.0,
     'b_sinks_2': 200.0}
    for name, (base, spread) in spreads.items():
        noise = np.random.default_rng([zlib.crc32(name.encode()), seed]).standard_normal(out[name].shape)
        drawn = base * np.exp(spread * noise) if base else spread * noise
        out[name] = __import__('jax').numpy.asarray(drawn.astype(out[name].dtype))
    for name, factor in factors.items():
        out[name] = (out[name] * factor).astype(out[name].dtype)
    return out
```

```python
from contextlib import ExitStack

import numpy as np

import concourse.bass as bass
from concourse import mybir

F32 = mybir.dt.float32
F32R = mybir.dt.float32r
U8 = mybir.dt.uint8
ALU = mybir.AluOpType
ACT = mybir.ActivationFunctionType
AX = mybir.AxisListType.X

P = 128
SEQ = 256
NT = SEQ // P
D = 1024
KT = D // P
EPS = 1e-6
GN_EPS = 64e-5
HD = 64
DFF = 2816
MLP = 4096
IDX_HEADS = 8
A_HEADS = 8
TOPK = SEQ // 4
CONV = 512
X_HEADS = 4
XHD = D // X_HEADS
R_HEADS = D // HD
RAW_SLOTS = 6
SPLIT_SLOTS = 6
BIG = 1.0e30
NONCAUSAL = -3.0e38
TAKEN = -3.4e38
DECAY = float(np.exp(-0.5))

Q_A, K_A, V_A = 0, 512, 576
Q_I, K_I, W_I = 640, 1152, 1216
GATE_B, GATE_C, CONV_IN, G_A, G_B = 1224, 1736, 2248, 2760, 3784

GAINS = {}
_at = 0
for _n, _rows in (("ffn1_pre", 8), ("mix_pre", 8), ("mem", 8), ("xattn_pre", 8), ("ffn2_pre", 8), ("ln_mix", 16),
                  ("ln_mlp", 16), ("kv_norm", 8), ("conv", 12), ("pad", 4), ("mu", 48)):
    GAINS[_n] = _at
    _at += _rows
GAIN_ROWS = _at
GAIN_SPLIT = GAINS["pad"]

CONSTS = {}
_at = 0
for _n, _w in (("ident", 128), ("cos", 64), ("sin", 64), ("causal", 384), ("invalid", 384), ("dist", 384), ("tri", 128),
               ("ends", 2), ("upper", 512), ("lower", 128)):
    CONSTS[_n] = (_at, _w)
    _at += _w
N_CONST = _at
LEVELS = 6


def shape_constants():
    c = np.zeros((P, N_CONST), np.float32)

    def put(name, a):
        at, w = CONSTS[name]
        c[:, at:at + w] = a.reshape(P, w)

    i = np.arange(P)
    eye = np.eye(P, dtype=np.float32)
    put("ident", eye)
    inv = np.float32(10000.0) ** (-np.arange(0, HD, 2, dtype=np.float32) / np.float32(HD))
    ang = np.arange(SEQ, dtype=np.float32)[:, None] * inv[None, :]
    put("cos", np.cos(ang).reshape(NT, P, 32).transpose(1, 0, 2).astype(np.float32))
    put("sin", np.sin(ang).reshape(NT, P, 32).transpose(1, 0, 2).astype(np.float32))
    q = np.concatenate([np.repeat(i[:, None], P, 1), np.repeat(i[:, None] + P, SEQ, 1)], 1)
    k = np.concatenate([np.arange(P), np.arange(SEQ)])[None, :]
    put("causal", (k <= q).astype(np.float32))
    put("invalid", np.where(k <= q, 0.0, NONCAUSAL).astype(np.float32))
    dist = q - k
    put("dist", np.where((dist >= 0) & (dist < P), dist, BIG).astype(np.float32))
    s, t = i[:, None], i[None, :]
    put("tri", (s <= t).astype(np.float32) - (s < P // 2).astype(np.float32))
    put("ends", np.stack([(i >= P // 2), (i < P // 2)], 1).astype(np.float32))
    strict, full = (s < t).astype(np.float32), (s <= t).astype(np.float32)
    put("upper", np.stack([strict, full, strict, full], 1).astype(np.float32))
    put("lower", strict.T.astype(np.float32))
    lev = np.zeros((P, 2, LEVELS + 1, P), np.float32)
    for n in range(LEVELS + 1):
        b = 2 ** n
        m = (s // (2 * b) == t // (2 * b)) & (s // b < t // b)
        lev[:, 0, n], lev[:, 1, n] = m, m.T
    return c, lev.reshape(P, -1)


class Lane:

    def __init__(self, eng, results):
        self.e, self.results, self.reached, self.last = eng, results, {}, None

    def one(self, sem=None):
        sem = self.results if sem is None else sem
        if isinstance(sem, Later):
            sem = sem.sem
        self.reached[sem.name] = self.reached.get(sem.name, 0) + 1
        self.last = (sem, self.reached[sem.name])
        return sem, 1


class Later:

    def __init__(self, sem, before):
        self.sem, self.before = sem, before


def stage(sem, n):
    return (sem.sem, sem.before + n) if isinstance(sem, Later) else (sem, n)


class Plan:

    def __init__(self):
        self.src, self.raw, self.split, self.raw_before, self.split_before, self.load_count = [], [], [], [], [], []
        self.raw_last, self.split_last = {}, {}
        self.uses = [0] * RAW_SLOTS

    def add(self, src, raw, split):
        c = len(self.src)
        self.src.append(src)
        self.raw.append(raw)
        self.split.append(split)
        self.raw_before.append(self.raw_last.get(raw))
        self.split_before.append(self.split_last.get(split))
        self.raw_last[raw], self.split_last[split] = c, c
        self.uses[raw] += 1
        self.load_count.append(self.uses[raw])
        return c


def build(nc, a, out):
    with ExitStack() as ctx:
        def sb(name, shape, dt=F32):
            return ctx.enter_context(nc.sbuf_tensor("sb_" + name, shape, dt))

        def ps(name, shape):
            return ctx.enter_context(nc.psum_tensor(name, shape, F32))

        def sem(name):
            return ctx.enter_context(nc.semaphore(name))

        raw = sb("raw", [P, RAW_SLOTS, 2, 512])
        w_hi = sb("w_hi", [P, SPLIT_SLOTS, 2, 512], F32R)
        w_lo = sb("w_lo", [P, SPLIT_SLOTS, 2, 512], F32R)
        xa_hi, xa_lo = sb("xa_hi", [P, KT, SEQ], F32R), sb("xa_lo", [P, KT, SEQ], F32R)
        xb_hi, xb_lo = sb("xb_hi", [P, KT, SEQ], F32R), sb("xb_lo", [P, KT, SEQ], F32R)
        mid_hi, mid_lo = sb("mid_hi", [P, 4, SEQ], F32R), sb("mid_lo", [P, 4, SEQ], F32R)
        XA, XB, MID = (xa_hi, xa_lo), (xb_hi, xb_lo), (mid_hi, mid_lo)
        h = sb("h", [P, NT, D])
        consts = sb("consts", [P, N_CONST])
        levels = sb("levels", [P, 2, LEVELS + 1, P], U8)
        gains = sb("gains", [P, GAIN_ROWS])
        gain_b = [sb(f"gain_b{n}", [P, D]) for n in range(2)]
        arena = [sb(f"arena{n}", [P, NT * D]) for n in range(8)]
        stat = sb("stat", [P, 512])
        half = sb("half", [P, 1])
        acc = ps("acc", [P, NT, D])
        gp = ps("gp", [P, NT, 512])
        tp = ps("tp", [P, 2, 512])

        def const(name):
            at, w = CONSTS[name]
            return consts[:, at:at + w]

        ident = const("ident")

        def rows(slot):
            return arena[slot][:, :].rearrange("p (t d) -> p t d", t=NT)

        def cols(slot):
            return arena[slot][:, :].rearrange("p (k s) -> p k s", s=SEQ)

        raw_loaded = [sem(f"raw_loaded{n}") for n in range(RAW_SLOTS)]
        hi_done, lo_done, chunk_used = sem("hi_done"), sem("lo_done"), sem("chunk_used")
        act_results, dve_results, pe_results, pool_results = (sem(x + "_results") for x in ("act", "dve", "pe", "pool"))
        consts_loaded, gains_ready, half_ready = sem("consts_loaded"), sem("gains_ready"), sem("half_ready")
        out_stored, levels_loaded = sem("out_stored"), sem("levels_loaded")

        plan = Plan()

        def load_chunk(sp, c):
            if plan.raw_before[c] is not None:
                sp.wait_ge(lo_done, plan.raw_before[c] + 1)
            s = plan.raw[c]
            for dst, src in plan.src[c](raw[:, s]):
                sp.dma_start(dst, src).then_inc(raw_loaded[s], 16)

        def two_rows(w, k, c0, n, wide=None):
            def src(slot):
                return [(slot[:, j, 0:n], w[(k + j) * P:(k + j + 1) * P, c0:c0 + n]) for j in range(2)]
            return src

        split_next = {"hi": 0, "lo": 0}

        def split_hi(A, upto):
            while split_next["hi"] < min(upto, len(plan.src)):
                c = split_next["hi"]
                split_hi_one(A, c, raw_loaded[plan.raw[c]], 32 * plan.load_count[c],
                             None if plan.split_before[c] is None else plan.split_before[c] + 1, plan.raw[c], plan.split[c])
                split_next["hi"] += 1

        def split_hi_one(A, c, loaded, loaded_n, used_n, r, s):
            A.e.wait_ge(loaded, loaded_n)
            if used_n is not None:
                A.e.wait_ge(chunk_used, used_n)
            A.e.activation(w_hi[:, s], raw[:, r], ACT.Copy).then_inc(hi_done, 1)

        def split_lo(V, upto):
            while split_next["lo"] < min(upto, len(plan.src)):
                c = split_next["lo"]
                split_lo_one(V, c, plan.raw[c], plan.split[c])
                split_next["lo"] += 1

        def split_lo_one(V, c, r, s):
            V.e.wait_ge(hi_done, c + 1)
            V.e.tensor_tensor(w_lo[:, s], raw[:, r], w_hi[:, s].bitcast(F32), ALU.subtract).then_inc(lo_done, 1)

        def product(e, dst, x, k, t, s, j, c0, n, start, stop):
            xh, xl = x[0][:, k, t * P:(t + 1) * P], x[1][:, k, t * P:(t + 1) * P]
            wh, wl = w_hi[:, s, j, c0:c0 + n], w_lo[:, s, j, c0:c0 + n]
            e.matmul(dst, xh, wh, start=start, stop=False)
            e.matmul(dst, xl, wh, start=False, stop=False)
            return e.matmul(dst, xh, wl, start=False, stop=stop)

        class Product:

            def __init__(self, w, kts, blocks):
                self.blocks, self.kts, self.first = blocks, kts, []
                for c0, n in blocks:
                    self.first.append(len(plan.src))
                    for k in range(0, kts, 2):
                        c = len(plan.src)
                        plan.add(two_rows(w, k, c0, n), c % RAW_SLOTS, c % SPLIT_SLOTS)
                self.end = len(plan.src)

            def last(self, b):
                return self.first[b] + self.kts // 2

            def pe(self, T, b, x, dst, ready, free=None):
                if ready is not None:
                    T.e.wait_ge(*stage(*ready))
                if free is not None:
                    T.e.wait_ge(*stage(*free))
                n = self.blocks[b][1]
                for m in range(self.kts // 2):
                    c = self.first[b] + m
                    T.e.wait_ge(lo_done, c + 1)
                    for t in range(NT):
                        for j in range(2):
                            k = 2 * m + j
                            mm = product(T.e, dst(t)[:, 0:n], x, k, t, plan.split[c], j, 0, n, k == 0, k == self.kts - 1)
                    mm.then_inc(chunk_used, 1)

        stat_at = [0]

        def stats(n):
            at = stat_at[0]
            stat_at[0] += n
            assert stat_at[0] <= 512
            return stat[:, at:at + n]

        class Rms:

            squared, mean, ready = sem("norm_squared"), sem("norm_mean"), sem("norm_rstd")

            def __init__(self):
                self.st = stats(2)

            def start(self, n):
                self.n = n

            def act(self, A, src, junk, wait):
                for t in range(NT):
                    A.e.wait_ge(*wait)
                    A.e.activation(junk, src(t), ACT.Square, accum_out=self.st[:, t:t + 1]).then_inc(*A.one(self.squared))
                    A.e.wait_ge(*A.last)

            def dve(self, V):
                V.e.wait_ge(self.squared, NT * (self.n + 1))
                V.e.tensor_scalar(self.st, self.st, 1.0 / D, EPS, ALU.mult, ALU.add).then_inc(*V.one(self.mean))

            def pool(self, G):
                G.e.wait_ge(half_ready, 1)
                G.e.wait_ge(self.mean, self.n + 1)
                G.e.tensor_tensor(self.st, self.st, half[:, 0:1].to_broadcast([P, 2]), ALU.pow).then_inc(*G.one(self.ready))

        class ToColumns:

            turned, hi, done, done_plain = sem("turned"), sem("cols_hi"), sem("cols_done"), sem("plain_cols_done")

            def __init__(self, kts=KT, plain=False):
                self.kts, self.plain = kts, plain

            def start(self, before):
                self.turned0 = sum(x.kts // 2 for x in before)
                self.hi0 = sum(x.kts for x in before if not x.plain)
                self.done0 = sum(x.kts for x in before if x.plain == self.plain)

            def done_at(self, k):
                return (self.done_plain if self.plain else self.done, self.done0 + k)

            def complete(self):
                return self.done_at(self.kts)

            def pe(self, T, src, ready):
                T.e.wait_ge(*stage(*ready))
                for n in range(self.kts // 2):
                    if n >= 2:
                        T.e.wait_ge(*self.done_at(2 * (n - 1)))
                    for j in range(2):
                        for t in range(NT):
                            at = (2 * j + t) * P
                            mm = T.e.transpose(tp[:, n % 2, at:at + P], src(2 * n + j, t), ident)
                    mm.then_inc(*T.one(self.turned))

            def act(self, A, x, gain=None, free=None):
                if free is not None:
                    A.e.wait_ge(*free)
                for k in range(self.kts):
                    A.e.wait_ge(self.turned, self.turned0 + k // 2 + 1)
                    src = tp[:, (k // 2) % 2, (k % 2) * SEQ:(k % 2 + 1) * SEQ]
                    scale = 1.0 if gain is None else gains[:, gain + k:gain + k + 1]
                    A.e.activation(x[0][:, k, :], src, ACT.Copy, scale=scale).then_inc(*A.one(self.hi))

            def dve(self, V, x, gain=None):
                for k in range(self.kts):
                    V.e.wait_ge(self.hi, self.hi0 + 2 * (k // 2 + 1))
                    src = tp[:, (k // 2) % 2, (k % 2) * SEQ:(k % 2 + 1) * SEQ]
                    scale = 1.0 if gain is None else gains[:, gain + k:gain + k + 1]
                    V.e.scalar_tensor_tensor(x[1][:, k, :], src, scale, x[0][:, k, :].bitcast(F32), ALU.mult, ALU.subtract).then_inc(*V.one(self.done))

            def act_plain(self, A, x, gain):
                for k in range(self.kts):
                    A.e.wait_ge(self.turned, self.turned0 + k // 2 + 1)
                    src = tp[:, (k // 2) % 2, (k % 2) * SEQ:(k % 2 + 1) * SEQ]
                    scale = 1.0 if gain is None else gains[:, gain + k:gain + k + 1]
                    A.e.activation(x[:, k, :], src, ACT.Copy, scale=scale).then_inc(*A.one(self.done_plain))

        class PreNorm:

            scaled = sem("norm_scaled")

            def __init__(self, gain, scratch, x):
                self.rms, self.turn = Rms(), ToColumns(plain=x is None)
                self.gain, self.scratch, self.x = gain, scratch, x

            def act(self, A, src, ready, free=None, plain=None):
                self.rms.act(A, src, rows(self.scratch)[:, 0, :], ready)
                if plain is None:
                    self.turn.act(A, self.x, self.gain, free)
                else:
                    self.turn.act_plain(A, plain, self.gain)

            def dve(self, V, src, plain=False):
                self.rms.dve(V)
                V.e.wait_ge(self.rms.ready, self.rms.n + 1)
                V.e.wait_ge(*V.last)
                for t in range(NT):
                    V.e.tensor_scalar(rows(self.scratch)[:, t, :], src(t), self.rms.st[:, t:t + 1], None, ALU.mult).then_inc(*V.one(self.scaled))
                if not plain:
                    self.turn.dve(V, self.x, self.gain)

            def start(self, n):
                self.n = n

            def pool(self, G):
                self.rms.pool(G)

            def pe(self, T):
                self.turn.pe(T, lambda k, t: rows(self.scratch)[:, t, k * P:(k + 1) * P], (self.scaled, NT * (self.n + 1)))

        class PostNorm:

            gain_loaded, acc_free, h_done = sem("post_gain_loaded"), sem("post_acc_free"), sem("post_h_done")

            def __init__(self, g, factor, scratch, b):
                self.rms = Rms()
                self.g, self.factor, self.scratch, self.b = g, factor, scratch, b

            def start(self, n):
                self.n = n
                self.freed, self.done = (self.acc_free, NT * (n + 1)), (self.h_done, NT * (n + 1))

            def sp(self, sp, wait=None):
                if wait is not None:
                    sp.wait_ge(*wait)
                sp.dma_start(gain_b[self.b][:, :], self.g.partition_broadcast(P)).then_inc(self.gain_loaded, 16)

            def act(self, A, ready):
                self.rms.act(A, lambda t: acc[:, t, :], rows(self.scratch)[:, 0, :], ready)

            def pool(self, G):
                self.rms.pool(G)

            def dve(self, V):
                self.rms.dve(V)
                V.e.wait_ge(self.rms.ready, self.rms.n + 1)
                V.e.wait_ge(self.gain_loaded, 16 * (self.n + 1))
                for t in range(NT):
                    V.e.scalar_tensor_tensor(rows(self.scratch)[:, t, :], acc[:, t, :], self.rms.st[:, t:t + 1],
                                                  gain_b[self.b][:, :], ALU.mult, ALU.mult).then_inc(*V.one(self.acc_free))
                for t in range(NT):
                    V.e.wait_ge(*V.last)
                    V.e.scalar_tensor_tensor(h[:, t, :], rows(self.scratch)[:, t, :], self.factor, h[:, t, :],
                                                  ALU.mult, ALU.add).then_inc(*V.one(self.h_done))

        class FeedForward:

            acted, made = sem("mid_acted"), sem("mid_made")
            mid_turned, mid_hi, mid_cols = sem("mid_turned"), sem("mid_hi"), sem("mid_cols")

            def __init__(self, up, gate, down, total, x, scratch):
                self.gated = gate is not None
                self.wide = 256 if self.gated else 512
                self.up, self.gate, self.down, self.x = up, gate, down, x
                self.trips = total // self.wide
                self.tiles = self.wide // P
                self.banks = self.tiles // 2
                self.ups = KT // 2
                self.period = self.ups + self.tiles
                self.split_ring = 6 if self.gated else 4
                self.raw_ring = 6 if self.gated else 4
                self.c0 = len(plan.src)
                for i in range(self.trips + 1):
                    if i < self.trips:
                        for m in range(self.ups):
                            plan.add(self.up_src(i, m), m % self.raw_ring, m % self.split_ring)
                    if i > 0:
                        for m in range(self.tiles):
                            plan.add(self.down_src(i - 1, m), (self.ups + m) % self.raw_ring, (self.ups + m) % self.split_ring)
                self.end = len(plan.src)
                self.mid_rows = rows(scratch)
                self.silu = rows(scratch)[:, :, 512:1024]

            def start_counts(self, before):
                self.rows0 = sum(NT * x.trips for x in before)
                self.banks0 = sum(x.banks * x.trips for x in before)

            def up_src(self, i, m):
                def src(slot):
                    if self.gated:
                        at = [w[2 * m * P:(2 * m + 2) * P, bass.ds(i * self.wide, self.wide)].rearrange("(k p) n -> p k n", p=P)
                              for w in (self.up, self.gate)]
                        return [(slot[:, :, n * 256:(n + 1) * 256], at[n]) for n in range(2)]
                    return [(slot[:, j, :], self.up[(2 * m + j) * P:(2 * m + j + 1) * P, bass.ds(i * self.wide, self.wide)])
                            for j in range(2)]
                return src

            def down_src(self, i, m):
                def src(slot):
                    at = self.down[bass.ds(i * self.wide + m * P, P), :]
                    return [(slot[:, n, :], at[:, n * 512:(n + 1) * 512]) for n in range(2)]
                return src

            def start(self, i):
                if isinstance(i, int) and i == 0:
                    return self.c0
                return self.c0 + self.ups + (i - 1) * self.period

            def sp(self, sp, upto_hook=None):
                for c in range(self.c0, self.c0 + self.ups + self.period):
                    load_chunk(sp, c)
                with sp.Fori(2, self.trips) as i:
                    base = self.start(i)
                    for m in range(self.period):
                        s = m % self.raw_ring
                        c = base + m
                        sp.wait_ge(lo_done, c - self.raw_ring + 1)
                        src = self.up_src(i, m) if m < self.ups else self.down_src(i - 1, m - self.ups)
                        for dst, at in src(raw[:, s]):
                            sp.dma_start(dst, at).then_inc(raw_loaded[s], 16)
                for c in range(self.end - self.tiles, self.end):
                    load_chunk(sp, c)

            def loads(self, i, m):
                one = self.start(1) + m
                return plan.load_count[one] + (i - 1) * (self.period // self.raw_ring)

            def hi_one(self, A, i, m):
                c = self.start(i) + m
                s = m % self.split_ring
                split_hi_one(A, c, raw_loaded[m % self.raw_ring], self.loads(i, m) * 32, c - self.split_ring + 1, m % self.raw_ring, s)

            def lo_one(self, V, i, m):
                split_lo_one(V, self.start(i) + m, m % self.raw_ring, m % self.split_ring)

            def act_middle(self, A, i):
                A.e.wait_ge(chunk_used, self.start(i) + self.ups)
                if_first = isinstance(i, int) and i == 0
                if not if_first:
                    A.e.wait_ge(self.made, self.rows0 + NT * i)
                for t in range(NT):
                    if self.gated:
                        A.e.activation(self.silu[:, t, 0:256], gp[:, t, 0:256], ACT.Silu).then_inc(self.acted, 1)
                    else:
                        A.e.activation(self.silu[:, t, :], gp[:, t, :], ACT.Relu).then_inc(self.acted, 1)

            def dve_middle(self, V, i):
                if not (isinstance(i, int) and i == 0):
                    V.e.wait_ge(self.mid_turned, self.banks0 + self.banks * i)
                for t in range(NT):
                    V.e.wait_ge(self.acted, self.rows0 + NT * i + t + 1)
                    if self.gated:
                        V.e.tensor_tensor(self.mid_rows[:, t, 0:256], self.silu[:, t, 0:256], gp[:, t, 256:512], ALU.mult).then_inc(self.made, 1)
                    else:
                        V.e.tensor_tensor(self.mid_rows[:, t, 0:512], self.silu[:, t, :], self.silu[:, t, :], ALU.mult).then_inc(self.made, 1)

            def turn_out(self, lane, i, high):
                for b in range(self.banks):
                    dst = MID[0 if high else 1][:, 2 * b:2 * b + 2, :].rearrange("p k s -> p (k s)")
                    if high:
                        lane.e.wait_ge(self.mid_turned, self.banks0 + self.banks * i + b + 1)
                        lane.e.activation(dst, tp[:, b, :], ACT.Copy).then_inc(self.mid_hi, 1)
                    else:
                        lane.e.wait_ge(self.mid_hi, self.banks0 + self.banks * i + b + 1)
                        hi = MID[0][:, 2 * b:2 * b + 2, :].rearrange("p k s -> p (k s)").bitcast(F32)
                        lane.e.tensor_tensor(dst, tp[:, b, :], hi, ALU.subtract).then_inc(self.mid_cols, 1)

            def pe_up(self, T, i, m0=0):
                if not (isinstance(i, int) and i == 0):
                    T.e.wait_ge(self.made, self.rows0 + NT * i)
                for m in range(self.ups):
                    T.e.wait_ge(lo_done, self.start(i) + m + 1)
                    for t in range(NT):
                        for j in range(2):
                            k = 2 * m + j
                            mm = product(T.e, gp[:, t, :], self.x, k, t, m % self.split_ring, j, 0, 512, k == 0, k == KT - 1)
                    mm.then_inc(chunk_used, 1)

            def pe_down(self, T, i, first, last):
                T.e.wait_ge(self.mid_cols, self.banks0 + self.banks * (i + 1))
                for m in range(self.tiles):
                    c = self.end - self.tiles + m if last else self.start(i + 1) + self.ups + m
                    T.e.wait_ge(lo_done, c + 1)
                    s = (self.ups + m) % self.split_ring
                    for t in range(NT):
                        for n in range(2):
                            mm = product(T.e, acc[:, t, n * 512:(n + 1) * 512], MID, m, t, s, n, 0, 512,
                                         first and m == 0, last and m == self.tiles - 1)
                    mm.then_inc(chunk_used, 1)

            def pe_turn(self, T, i):
                T.e.wait_ge(self.made, self.rows0 + NT * (i + 1))
                if not (isinstance(i, int) and i == 0):
                    T.e.wait_ge(self.mid_cols, self.banks0 + self.banks * i)
                for b in range(self.banks):
                    for j in range(2):
                        for t in range(NT):
                            at = (2 * b + j) * P
                            mm = T.e.transpose(tp[:, b, (2 * j + t) * P:(2 * j + t + 1) * P], self.mid_rows[:, t, at:at + P], ident)
                    mm.then_inc(self.mid_turned, 1)

            def pe(self, T, ready, acc_free=None):
                T.e.wait_ge(*stage(*ready))
                self.pe_up(T, 0)
                self.pe_turn(T, 0)
                if acc_free is not None:
                    T.e.wait_ge(*acc_free)
                self.pe_up(T, 1)
                self.pe_down(T, 0, True, False)
                self.pe_turn(T, 1)
                with T.e.Fori(2, self.trips) as i:
                    self.pe_up(T, i)
                    self.pe_down(T, i - 1, False, False)
                    self.pe_turn(T, i)
                self.pe_down(T, self.trips - 1, False, True)

            def lane(self, L, upto, one, middle, out):
                upto(L, self.c0 + self.ups)
                middle(L, 0)
                upto(L, self.start(1) + self.ups)
                out(L, 0)
                self.in_order(L, lambda lo, hi: upto(L, self.start(1) + hi), 1, middle)
                with L.e.Fori(2, self.trips) as i:
                    for m in range(self.ups):
                        one(L, i, m)
                    out(L, i - 1)
                    self.in_order(L, lambda lo, hi: [one(L, i, m) for m in range(lo, hi)], i, middle)
                out(L, self.trips - 1)

            def in_order(self, L, splits, i, middle):
                splits(self.ups, self.period)
                middle(L, i)

            def act(self, A):
                self.lane(A, split_hi, self.hi_one, self.act_middle, lambda L, i: self.turn_out(L, i, True))
                split_next["hi"] = self.end - self.tiles

            def dve(self, V):
                self.lane(V, split_lo, self.lo_one, self.dve_middle, lambda L, i: self.turn_out(L, i, False))
                split_next["lo"] = self.end - self.tiles


        x_loaded = sem("x_loaded")
        gains_loaded = sem("gains_loaded")
        gain_rows = [rows(7)[:, 0, 0:P], rows(7)[:, 0, P:2 * P]]
        gains_turned = sem("gains_turned")

        class SetUp:
            def sp(self, sp):
                for t in range(NT):
                    sp.dma_start(h[:, t, :], a["x"][0, t * P:(t + 1) * P, :]).then_inc(x_loaded, 16)
                sp.dma_start(consts[:, :], a["consts"]).then_inc(consts_loaded, 16)
                vectors = [("ffn1_pre", a["ffn1_pre_g"]), ("mix_pre", a["mix_pre_g"]), ("mem", a["mem_g"]),
                           ("xattn_pre", a["xattn_pre_g"]), ("ffn2_pre", a["ffn2_pre_g"]), ("ln_mix", a["ln_mix_2"]),
                           ("ln_mlp", a["ln_mlp_2"]), ("conv", a["conv_w"][0])]
                for name, v in vectors:
                    v = v.rearrange("a (k p) -> (a k) p", p=P)
                    at = GAINS[name]
                    sp.dma_start(gain_rows[0][at:at + v.shape[0], :], v).then_inc(gains_loaded, 16)
                at = GAINS["kv_norm"]
                sp.dma_start(gain_rows[0][at:at + 8, :], a["kv_norm_2"].rearrange("(k p) -> k p", p=P)).then_inc(gains_loaded, 16)
                sp.dma_start(gain_rows[1][0:48, :], a["a_mu_2"][0].rearrange("a (k p) -> (a k) p", p=P)).then_inc(gains_loaded, 16)
                self.n = 16 * (len(vectors) + 2)
                sp.dma_start(flat(0, 0, 2 * (LEVELS + 1) * P), a["levels"]).then_inc(levels_loaded, 16)

            def pe(self, T):
                T.e.wait_ge(consts_loaded, 16)
                T.e.wait_ge(gains_loaded, 160)
                n = GAIN_SPLIT
                T.e.transpose(tp[:, 0, 0:n], gain_rows[0][0:n, :], ident[0:n, 0:n]).then_inc(*T.one(gains_turned))
                T.e.transpose(tp[:, 0, n:n + 48], gain_rows[1][0:48, :], ident[0:48, 0:48]).then_inc(*T.one(gains_turned))

            def act(self, A):
                A.e.wait_ge(gains_turned, 2)
                n = GAIN_SPLIT
                A.e.activation(gains[:, 0:n], tp[:, 0, 0:n], ACT.Copy).then_inc(*A.one(gains_ready))
                A.e.activation(gains[:, GAINS["mu"]:GAINS["mu"] + 48], tp[:, 0, n:n + 48], ACT.Copy).then_inc(*A.one(gains_ready))
                A.e.wait_ge(*A.last)

            def dve(self, V):
                V.e.wait_ge(consts_loaded, 16)
                V.e.wait_ge(gains_ready, 2)

            def dve_levels(self, V):
                V.e.wait_ge(levels_loaded, 16)
                V.e.tensor_copy(levels[:, :, :, :].rearrange("p a l s -> p (a l s)"), flat(0, 0, 2 * (LEVELS + 1) * P)).then_inc(*V.one())

            def pool(self, G):
                G.e.memset(half[:, :], -0.5).then_inc(*G.one(half_ready))

        setup = SetUp()

        def h_rows(t):
            return h[:, t, :]

        w = {n: a[n][0] for n in ("ffn1_w1", "ffn1_w3", "ffn1_w2", "w_in", "w_a_out", "w_b_out", "w_out", "xattn_w_q",
                                  "xattn_w_kv", "xattn_w_o", "ffn2_w1", "ffn2_w3", "ffn2_w2")}

        ffn1_pre = PreNorm(GAINS["ffn1_pre"], 6, XA)
        ffn1 = FeedForward(w["ffn1_w1"], w["ffn1_w3"], w["ffn1_w2"], DFF, XA, 5)
        ffn1_post = PostNorm(a["ffn1_post_g"][0], 0.5, 6, 0)

        def flat(slot, at, n):
            return arena[slot][:, at:at + n]

        class Mix:
            BLOCKS = [(0, 512), (512, 512), (1024, 200), (GATE_C, 512), (CONV_IN, 512), (GATE_B, 512),
                      (G_A, 512), (G_A + 512, 512), (G_B, 512), (G_B + 512, 512)]

            def __init__(self):
                n = "mix_"
                self.pre = PreNorm(GAINS["mix_pre"], 6, XA)
                self.proj = Product(w["w_in"], KT, self.BLOCKS)
                self.yb = Product(w["w_b_out"], 4, [(0, 512), (512, 512)])
                self.ya = Product(w["w_a_out"], 4, [(0, 512), (512, 512)])
                self.out = Product(w["w_out"], KT, [(0, 512), (512, 512)])
                self.merge = ToColumns()
                self.post = PostNorm(a["mix_post_g"][0], 1.0, 0, 1)
                self.taken, self.roped, self.turned, self.columns = sem(n + "taken"), sem(n + "roped"), sem(n + "turned"), sem(n + "columns")
                self.relu_in, self.relu, self.scored, self.masked = sem(n + "relu_in"), sem(n + "relu"), sem(n + "scored"), sem(n + "masked")
                self.logit, self.biased, self.maxed, self.exped = sem(n + "logit"), sem(n + "biased"), sem(n + "maxed"), sem(n + "exped")
                self.normed, self.p_turned, self.p_columns, self.o = sem(n + "normed"), sem(n + "p_turned"), sem(n + "p_columns"), sem(n + "o")
                self.o_hi, self.o_done, self.m_rows, self.m_turned = sem(n + "o_hi"), sem(n + "o_done"), sem(n + "m_rows"), sem(n + "m_turned")
                self.m_cols, self.gate_turned, self.yb_f32, self.yb_hi = sem(n + "m_cols"), sem(n + "gate_turned"), sem(n + "yb_f32"), sem(n + "yb_hi")
                self.yb_done, self.merged, self.merged_b = sem(n + "yb_done"), sem(n + "merged"), sem(n + "merged_b")
                self.w_idx = stats(16)
                self.top = stats(8)
                self.sums = stats(16)
                self.neg_max = stats(16)
                self.values = flat(7, 1920, 128).rearrange("p (t d) -> p t d", t=NT)
                self.mask = flat(7, 1536, 384)
                self.key_cols = flat(7, 0, 512).rearrange("p (k s) -> p k s", k=2)
                self.z = flat(7, 512, 1024).rearrange("p (k s) -> p k s", k=4)
                self.q_cols = cols(2)
                self.gate_b = flat(3, 0, 1024).rearrange("p (t d) -> p t d", t=NT)
                self.gate_c = flat(3, 1024, 1024).rearrange("p (t d) -> p t d", t=NT)
                self.yb_cols = flat(3, 1024, 1024).rearrange("p (k s) -> p k s", k=4)
                self.m_row = flat(4, 0, 1024).rearrange("p (t d) -> p t d", t=NT)
                self.m_col = flat(4, 1024, 1024).rearrange("p (k s) -> p k s", k=4)
                self.relu_buf = [flat(6, 512 * n, 512) for n in range(2)]
                self.score = flat(6, 1024, 384)
                self.work = flat(6, 1408, 384)
                self.logits = [flat(1, 0, 8 * P).rearrange("p (h s) -> p h s", h=8), flat(0, 0, 8 * SEQ).rearrange("p (h s) -> p h s", h=8)]
                self.p_cols = [flat(4, 0, 8 * P).rearrange("p (c h q) -> p c h q", c=1, h=8), flat(2, 0, 16 * P).rearrange("p (c h q) -> p c h q", c=2, h=8)]

            KEYS = (P, 2 * P)
            TOGETHER = ((0, 2), (1, 3), (4, 6), (5, 7))
            MASK_AT = (0, P)

            def bank(self, b):
                return (lambda t: gp[:, t, :]) if b % 2 == 0 else (lambda t: acc[:, t, 0:512])

            def side(self, n):
                return acc[:, n % 2, 512:1024]

            def sp(self, sp):
                for c in range(self.proj.first[0], self.yb.first[0]):
                    load_chunk(sp, c)
                self.post.sp(sp)
                for c in range(self.yb.first[0], self.out.end):
                    load_chunk(sp, c)
                xattn.sp_memory(sp)

            def pool(self, G):
                self.pre.pool(G)

            TAKEN_AFTER = {0: 2, 1: 4, 2: 6, 3: 8, 5: 10, 6: 12, 7: 14, 8: 16, 9: 18}

            def bank_free(self, b):
                if b < 2:
                    return None
                return (self.m_rows, NT) if b == 6 else (self.taken, self.TAKEN_AFTER[b - 2])

            def pe_block(self, T, b):
                self.proj.pe(T, b, XA, self.bank(b), self.pre.turn.complete(), self.bank_free(b))

            def pe(self, T):
                self.pre.pe(T)
                for b in range(6):
                    self.pe_block(T, b)
                T.e.wait_ge(self.roped, 7)
                srcs = [(0, n * P) for n in range(4)] + [(0, 640 + n * P) for n in range(3)] + [(1, 0), (0, 512), (1, P)]
                for n in range(5):
                    if n >= 2:
                        T.e.wait_ge(self.columns, n - 1)
                    for j in range(2):
                        slot, at = srcs[2 * n + j]
                        for t in range(NT):
                            mm = T.e.transpose(tp[:, n % 2, (2 * j + t) * P:(2 * j + t + 1) * P], rows(slot)[:, t, at:at + P], ident)
                    mm.then_inc(*T.one(self.turned))
                T.e.wait_ge(self.m_rows, NT)
                for n in range(2):
                    T.e.wait_ge(self.columns, 4 + n)
                    for j in range(2):
                        for t in range(NT):
                            at = (2 * n + j) * P
                            mm = T.e.transpose(tp[:, (n + 1) % 2, (2 * j + t) * P:(2 * j + t + 1) * P], self.m_row[:, t, at:at + P], ident)
                    mm.then_inc(*T.one(self.m_turned))
                n = 0
                for t in range(NT):
                    for heads in self.TOGETHER:
                        if n >= 2:
                            T.e.wait_ge(self.relu, n - 1)
                        for j, head in enumerate(heads):
                            e = head % 2
                            q = self.q_cols[e * HD:(e + 1) * HD, 4 + head // 2, t * P:(t + 1) * P]
                            kk = self.key_cols[e * HD:(e + 1) * HD, 1, 0:self.KEYS[t]]
                            mm = T.e.matmul(self.side(n)[:, j * self.KEYS[t]:(j + 1) * self.KEYS[t]], q, kk, start=True, stop=True)
                        mm.then_inc(*T.one(self.relu_in))
                        n += 1
                T.e.wait_ge(self.taken, self.TAKEN_AFTER[5])
                for n in range(2):
                    T.e.wait_ge(self.m_cols, n + 1)
                    for j in range(2):
                        for t in range(NT):
                            at = (2 * n + j) * P
                            mm = T.e.transpose(tp[:, (n + 1) % 2, (2 * j + t) * P:(2 * j + t + 1) * P], self.gate_b[:, t, at:at + P], ident)
                    mm.then_inc(*T.one(self.gate_turned))
                self.pe_block(T, 6)
                self.pe_block(T, 7)
                n = 0
                for t in range(NT):
                    for heads in self.TOGETHER:
                        if n >= 2:
                            T.e.wait_ge(self.biased, 2 * (n - 1))
                        else:
                            T.e.wait_ge(self.relu, 8)
                        for j, head in enumerate(heads):
                            e = head % 2
                            q = self.q_cols[e * HD:(e + 1) * HD, head // 2, t * P:(t + 1) * P]
                            kk = self.key_cols[e * HD:(e + 1) * HD, 0, 0:self.KEYS[t]]
                            mm = T.e.matmul(self.side(n)[:, j * self.KEYS[t]:(j + 1) * self.KEYS[t]], q, kk, start=True, stop=True)
                        mm.then_inc(*T.one(self.logit))
                        n += 1
                T.e.wait_ge(self.scored, 16)
                self.pe_block(T, 8)
                self.pe_block(T, 9)
                T.e.wait_ge(self.yb_f32, 2)
                n = 0
                for t in range(NT):
                    T.e.wait_ge(self.normed, t + 1)
                    for c in range(t + 1):
                        for g in range(2):
                            if n >= 2:
                                T.e.wait_ge(self.p_columns, n - 1)
                            for j in range(4):
                                mm = T.e.transpose(tp[:, n % 2, j * P:(j + 1) * P], self.logits[t][:, 4 * g + j, c * P:(c + 1) * P], ident)
                            mm.then_inc(*T.one(self.p_turned))
                            n += 1
                for t in range(NT):
                    T.e.wait_ge(self.p_columns, 2 if t == 0 else 6)
                    for e in range(2):
                        for c in range(t + 1):
                            mm = T.e.matmul(self.side(t)[e * HD:(e + 1) * HD, :].rearrange("p (h q) -> p h q", h=4), self.values[:, c, :],
                                            self.p_cols[t][:, c, e::2, :], start=c == 0, stop=c == t)
                    mm.then_inc(*T.one(self.o))
                self.yb.pe(T, 0, (XB[0][:, 4:8], XB[1][:, 4:8]), lambda t: acc[:, t, 0:512], (self.yb_done, 1), (self.taken, 18))
                self.yb.pe(T, 1, (XB[0][:, 4:8], XB[1][:, 4:8]), lambda t: gp[:, t, :], (self.yb_done, 1))
                self.ya.pe(T, 0, XB, lambda t: tp[:, t, :], (self.o_done, NT), (self.p_columns, 6))
                self.ya.pe(T, 1, XB, lambda t: acc[:, t, 512:1024], (self.o_done, NT))
                T.e.wait_ge(self.merged_b, 4)
                self.merge.pe(T, lambda k, t: rows(5)[:, t, k * P:(k + 1) * P], (self.merged, 4))
                for b in range(2):
                    self.out.pe(T, b, XA, lambda t: acc[:, t, b * 512:(b + 1) * 512], self.merge.complete())

            def act_take(self, A, b, dst, func=ACT.Copy):
                split_hi(A, self.proj.last(b) + 5)
                A.e.wait_ge(chunk_used, self.proj.last(b))
                for t in range(NT):
                    A.e.activation(dst(t), self.bank(b)(t)[:, 0:self.BLOCKS[b][1]], func).then_inc(*A.one(self.taken))

            def act(self, A):
                self.pre.act(A, h_rows, ffn1_post.done)
                A.e.wait_ge(*self.pre.turn.complete())
                self.act_take(A, 0, lambda t: rows(0)[:, t, 0:512])
                split_hi(A, self.proj.last(1) + 5)
                A.e.wait_ge(chunk_used, self.proj.last(1))
                for t in range(NT):
                    A.e.activation(self.values[:, t, :], self.bank(1)(t)[:, V_A - 512:V_A - 512 + HD], ACT.Copy).then_inc(*A.one())
                    A.e.activation(rows(0)[:, t, 512:1024], self.bank(1)(t), ACT.Copy).then_inc(*A.one(self.taken))
                split_hi(A, self.proj.last(2) + 5)
                A.e.wait_ge(chunk_used, self.proj.last(2))
                for t in range(NT):
                    A.e.activation(self.w_idx[:, 8 * t:8 * t + 8], self.bank(2)(t)[:, W_I - 1024:W_I - 1024 + 8], ACT.Copy,
                                        scale=float(IDX_HEADS) ** -0.5).then_inc(*A.one())
                    A.e.activation(rows(1)[:, t, 0:192], self.bank(2)(t)[:, 0:192], ACT.Copy).then_inc(*A.one(self.taken))
                self.act_take(A, 3, lambda t: self.gate_c[:, t, :])
                self.act_take(A, 5, lambda t: self.gate_b[:, t, :])
                for n in range(5):
                    A.e.wait_ge(self.turned, n + 1)
                    dst = (self.q_cols[:, 2 * n:2 * n + 2, :] if n < 4 else self.key_cols).rearrange("p k s -> p (k s)")
                    A.e.activation(dst, tp[:, n % 2, :], ACT.Copy).then_inc(*A.one(self.columns))
                for n in range(2):
                    A.e.wait_ge(self.m_turned, n + 1)
                    A.e.activation(self.m_col[:, 2 * n:2 * n + 2, :].rearrange("p k s -> p (k s)"), tp[:, (n + 1) % 2, :], ACT.Copy).then_inc(*A.one(self.m_cols))
                n = 0
                for t in range(NT):
                    for _ in self.TOGETHER:
                        A.e.wait_ge(self.relu_in, n + 1)
                        if n >= 2:
                            A.e.wait_ge(self.scored, 2 * (n - 1))
                        width = 2 * self.KEYS[t]
                        A.e.activation(self.relu_buf[n % 2][:, 0:width], self.side(n)[:, 0:width], ACT.Relu, scale=float(HD) ** -0.5).then_inc(*A.one(self.relu))
                        n += 1
                for b, c in ((6, 0), (7, 512)):
                    self.act_take(A, b, lambda t: rows(5)[:, t, c:c + 512], ACT.Sigmoid)
                A.e.wait_ge(self.yb_f32, 2)
                A.e.activation(XB[0][:, 4:8, :], self.yb_cols, ACT.Copy).then_inc(*A.one(self.yb_hi))
                A.e.wait_ge(self.masked, NT)
                split_hi(A, self.proj.last(9) + 3)
                for b, c in ((8, 0), (9, 512)):
                    self.act_take(A, b, lambda t: rows(6)[:, t, c:c + 512], ACT.Sigmoid)
                for t in range(NT):
                    A.e.wait_ge(*stage(self.maxed, t + 1))
                    for hd in range(A_HEADS):
                        A.e.activation(self.logits[t][:, hd, :], self.logits[t][:, hd, :], ACT.Exp,
                                            bias=self.neg_max[:, 8 * t + hd:8 * t + hd + 1], accum_out=self.sums[:, 8 * t + hd:8 * t + hd + 1]).then_inc(*A.one(self.exped))
                n = 0
                for t in range(NT):
                    for c in range(t + 1):
                        for g in range(2):
                            A.e.wait_ge(*stage(self.p_turned, n + 1))
                            A.e.activation(self.p_cols[t][:, c, 4 * g:4 * g + 4, :].rearrange("p h q -> p (h q)"), tp[:, n % 2, :], ACT.Copy).then_inc(*A.one(self.p_columns))
                            n += 1
                for t in range(NT):
                    A.e.wait_ge(self.o, t + 1)
                    A.e.activation(XB[0][:, 0:4, t * P:(t + 1) * P], self.side(t).rearrange("p (h q) -> p h q", h=4), ACT.Copy).then_inc(*A.one(self.o_hi))
                split_hi(A, self.ya.end + 4)
                self.merge.act(A, XA)
                split_hi(A, self.out.end + 4)
                xattn.mem_pre.act(A, lambda t: rows(7)[:, t, :], (mem_loaded, 16))
                self.post.act(A, (chunk_used, self.out.end))

            def dve(self, V):
                self.pre.dve(V, h_rows)
                split_lo(V, self.proj.last(2) + 5)
                V.e.wait_ge(self.taken, 6)
                n_rope = 0
                for slot, c0, heads in ((0, 0, 9), (0, 640, 6), (1, 0, 3)):
                    for t in range(NT):
                        x = rows(slot)[:, t, c0:c0 + heads * HD].rearrange("p (h d) -> p h d", h=heads)
                        x1, x2 = x[:, :, 0:32], x[:, :, 32:64]
                        tmp = [flat(2, 512 * n, heads * 32).rearrange("p (h d) -> p h d", h=heads) for n in range(4)]
                        cs, sn = (const(m)[:, 32 * t:32 * t + 32].unsqueeze(1).to_broadcast([P, heads, 32]) for m in ("cos", "sin"))
                        V.e.wait_ge(*V.last)
                        for n, (u, v) in enumerate(((x1, cs), (x2, sn), (x2, cs), (x1, sn))):
                            V.e.tensor_tensor(tmp[n], u, v, ALU.mult).then_inc(*V.one())
                        V.e.wait_ge(*V.last)
                        V.e.tensor_tensor(x1, tmp[0], tmp[1], ALU.subtract).then_inc(*V.one())
                        V.e.tensor_tensor(x2, tmp[2], tmp[3], ALU.add).then_inc(*V.one(self.roped if t == 1 else None))
                    split_lo(V, split_next["lo"] + 2)
                V.e.wait_ge(*V.last)
                for t in range(NT):
                    V.e.tensor_copy(rows(0)[:, t, 576:640], rows(0)[:, t, 512:576]).then_inc(*V.one(self.roped))
                    V.e.tensor_copy(rows(1)[:, t, 192:256], rows(1)[:, t, 128:192]).then_inc(*V.one(self.roped))
                split_lo(V, self.proj.last(4) + 5)
                V.e.wait_ge(self.taken, 8)
                V.e.wait_ge(chunk_used, self.proj.last(4))
                for t in range(NT):
                    V.e.tensor_tensor(self.m_row[:, t, :], self.gate_c[:, t, :], self.bank(4)(t), ALU.mult).then_inc(*V.one(self.m_rows))
                split_lo(V, self.proj.last(5) + 5)
                V.e.wait_ge(self.m_cols, 2)
                for k in range(4):
                    tap = [gains[:, GAINS["conv"] + 4 * n + k:GAINS["conv"] + 4 * n + k + 1] for n in range(3)]
                    V.e.tensor_scalar(self.z[:, k, :], self.m_col[:, k, :], tap[2], None, ALU.mult).then_inc(*V.one())
                    for n in (1, 2):
                        V.e.wait_ge(*V.last)
                        V.e.scalar_tensor_tensor(self.z[:, k, n:SEQ], self.m_col[:, k, 0:SEQ - n], tap[2 - n], self.z[:, k, n:SEQ], ALU.mult, ALU.add).then_inc(*V.one())
                n = 0
                for t in range(NT):
                    keys = self.KEYS[t]
                    sc = self.score[:, self.MASK_AT[t]:self.MASK_AT[t] + keys]
                    for heads in self.TOGETHER:
                        V.e.wait_ge(self.relu, n + 1)
                        for e, head in enumerate(heads):
                            wt = self.w_idx[:, 8 * t + head:8 * t + head + 1]
                            r = self.relu_buf[n % 2][:, e * keys:(e + 1) * keys]
                            if head == 0:
                                V.e.tensor_scalar(sc, r, wt, None, ALU.mult).then_inc(*V.one(self.scored))
                            else:
                                V.e.wait_ge(*V.last)
                                V.e.scalar_tensor_tensor(sc, r, wt, sc, ALU.mult, ALU.add).then_inc(*V.one(self.scored))
                        n += 1
                V.e.wait_ge(*V.last)
                split_lo(V, self.proj.last(6) + 5)
                for n in range(2):
                    V.e.wait_ge(self.gate_turned, n + 1)
                    V.e.wait_ge(*V.last)
                    src = tp[:, (n + 1) % 2, :].rearrange("p (k s) -> p k s", k=2)
                    V.e.tensor_tensor(self.yb_cols[:, 2 * n:2 * n + 2, :], self.z[:, 2 * n:2 * n + 2, :], src, ALU.mult).then_inc(*V.one(self.yb_f32))
                V.e.wait_ge(self.yb_hi, 1)
                V.e.tensor_tensor(XB[1][:, 4:8, :], self.yb_cols, XB[0][:, 4:8, :].bitcast(F32), ALU.subtract).then_inc(*V.one(self.yb_done))
                for t in range(NT):
                    at, keys = self.MASK_AT[t], self.KEYS[t]
                    sc, wk, mk = (x[:, at:at + keys] for x in (self.score, self.work, self.mask))
                    V.e.tensor_tensor(wk, sc, const("causal")[:, at:at + keys], ALU.mult).then_inc(*V.one())
                    V.e.wait_ge(*V.last)
                    V.e.tensor_tensor(wk, wk, const("invalid")[:, at:at + keys], ALU.add).then_inc(*V.one())
                    for _ in range(TOPK // 8):
                        V.e.wait_ge(*V.last)
                        V.e.max(self.top, wk).then_inc(*V.one())
                        V.e.wait_ge(*V.last)
                        V.e.match_replace(wk, self.top, wk, TAKEN).then_inc(*V.one())
                    V.e.wait_ge(*V.last)
                    V.e.tensor_scalar(wk, wk, TAKEN, None, ALU.is_equal).then_inc(*V.one())
                    V.e.wait_ge(*V.last)
                    V.e.tensor_tensor(wk, wk, const("causal")[:, at:at + keys], ALU.mult).then_inc(*V.one())
                    V.e.wait_ge(*V.last)
                    V.e.tensor_scalar(mk, wk, -1.0, BIG, ALU.add, ALU.mult).then_inc(*V.one(self.masked))
                    split_lo(V, min(split_next["lo"] + 3, self.proj.last(7) + 5))
                V.e.wait_ge(*V.last)
                split_lo(V, self.proj.last(7) + 5)
                n = 0
                for t in range(NT):
                    keys = self.KEYS[t]
                    for heads in self.TOGETHER:
                        V.e.wait_ge(*stage(self.logit, n + 1))
                        for e, head in enumerate(heads):
                            V.e.scalar_tensor_tensor(self.logits[t][:, head, :], self.side(n)[:, e * keys:(e + 1) * keys], float(HD) ** -0.5,
                                                          self.mask[:, self.MASK_AT[t]:self.MASK_AT[t] + keys], ALU.mult, ALU.add).then_inc(*V.one(self.biased))
                        n += 1
                for t in range(NT):
                    V.e.wait_ge(*V.last)
                    V.e.tensor_reduce(self.neg_max[:, 8 * t:8 * t + 8], self.logits[t], AX, ALU.max, negate=True).then_inc(*V.one(self.maxed))
                split_lo(V, self.proj.last(9) + 5)
                for t in range(NT):
                    V.e.wait_ge(self.exped, 8 * (t + 1))
                    s = self.sums[:, 8 * t:8 * t + 8]
                    V.e.reciprocal(s, s).then_inc(*V.one())
                    V.e.wait_ge(*V.last)
                    V.e.tensor_tensor(self.logits[t], self.logits[t], s.unsqueeze(2).to_broadcast([P, 8, self.KEYS[t]]), ALU.mult).then_inc(*V.one(self.normed))
                for t in range(NT):
                    V.e.wait_ge(self.o_hi, t + 1)
                    V.e.tensor_tensor(XB[1][:, 0:4, t * P:(t + 1) * P], self.side(t).rearrange("p (h q) -> p h q", h=4),
                                           XB[0][:, 0:4, t * P:(t + 1) * P].bitcast(F32), ALU.subtract).then_inc(*V.one(self.o_done))
                split_lo(V, self.ya.end + 4)
                V.e.wait_ge(self.taken, 18)
                for b, src in ((0, lambda t: acc[:, t, 0:512]), (1, lambda t: gp[:, t, :])):
                    V.e.wait_ge(chunk_used, self.yb.last(b))
                    for t in range(NT):
                        at = rows(6)[:, t, b * 512:(b + 1) * 512]
                        V.e.tensor_tensor(at, at, src(t), ALU.mult).then_inc(*V.one(self.merged_b))
                for b, src in ((0, lambda t: tp[:, t, :]), (1, lambda t: acc[:, t, 512:1024])):
                    V.e.wait_ge(chunk_used, self.ya.last(b))
                    for t in range(NT):
                        at = rows(5)[:, t, b * 512:(b + 1) * 512]
                        V.e.tensor_tensor(at, at, src(t), ALU.mult).then_inc(*V.one())
                for t in range(NT):
                    for b in range(2):
                        V.e.wait_ge(*V.last)
                        at = rows(5)[:, t, b * 512:(b + 1) * 512]
                        V.e.tensor_tensor(at, at, rows(6)[:, t, b * 512:(b + 1) * 512], ALU.add).then_inc(*V.one(self.merged))
                self.merge.dve(V, XA)
                split_lo(V, self.out.end + 4)
                xattn.mem_pre.dve(V, lambda t: rows(7)[:, t, :])
                self.post.dve(V)

        mix = Mix()

        mem_loaded = sem("mem_loaded")

        class MemoryAttention:

            def __init__(self):
                n = "xattn_"
                self.mem_pre = PreNorm(GAINS["mem"], 4, XB)
                self.kv = Product(w["xattn_w_kv"], KT, [(512 * b, 512) for b in range(4)])
                self.pre = PreNorm(GAINS["xattn_pre"], 5, XA)
                self.q = Product(w["xattn_w_q"], KT, [(0, 512), (512, 512)])
                self.out = Product(w["xattn_w_o"], KT, [(0, 512), (512, 512)])
                self.k_turn, self.q_turn = ToColumns(plain=True), ToColumns(plain=True)
                self.post = PostNorm(a["xattn_post_g"][0], 1.0, 0, 0)
                self.kv_taken, self.q_taken, self.logit = Later(mix.taken, 18), Later(mix.taken, 26), Later(mix.logit, 8)
                self.maxed, self.exped, self.normed = Later(mix.maxed, 2), Later(mix.exped, 16), Later(mix.normed, 2)
                self.p_turned, self.p_columns, self.o = Later(mix.p_turned, 6), Later(mix.p_columns, 6), Later(mix.o, 2)
                self.o_hi, self.o_done = Later(mix.o_hi, 2), Later(mix.o_done, 2)
                self.neg_max, self.sums = stats(8), stats(8)
                self.p_cols = arena[1][:, :].rearrange("p (c h q) -> p c h q", c=2, h=X_HEADS)
                self.probs = arena[6][:, :].rearrange("p (t h m) -> p t h m", t=NT, h=X_HEADS)

            def kv_bank(self, b):
                return (lambda t: gp[:, t, :], lambda t: tp[:, t, :], lambda t: acc[:, t, 0:512], lambda t: acc[:, t, 512:1024])[b]

            def sp_memory(self, sp):
                sp.wait_ge(mix.o, NT)
                sp.dma_start(rows(7), a["mem"][0].rearrange("(t p) d -> p t d", p=P)).then_inc(mem_loaded, 16)

            def sp(self, sp):
                for c in range(self.kv.first[0], self.kv.end):
                    load_chunk(sp, c)
                self.post.sp(sp, ffn1_post.freed)
                for c in range(self.q.first[0], self.out.end):
                    load_chunk(sp, c)

            def pe_memory(self, T):
                self.mem_pre.pe(T)
                frees = (None, None, mix.post.freed, mix.post.freed)
                for b in range(4):
                    self.kv.pe(T, b, XB, self.kv_bank(b), self.mem_pre.turn.complete(), frees[b])
                T.e.wait_ge(*stage(self.kv_taken, 4))
                self.k_turn.pe(T, lambda k, t: rows(1)[:, t, k * P:(k + 1) * P], (self.kv_taken, 4))

            def pe(self, T):
                T.e.wait_ge(*self.k_turn.complete())
                self.pre.pe(T)
                T.e.wait_ge(*stage(self.kv_taken, 8))
                for b in range(2):
                    self.q.pe(T, b, XA, lambda t: acc[:, t, b * 512:(b + 1) * 512], self.pre.turn.complete())
                self.q_turn.pe(T, lambda k, t: rows(6)[:, t, k * P:(k + 1) * P], (self.q_taken, 4))
                T.e.wait_ge(*self.q_turn.complete())
                n = 0
                for t in range(NT):
                    for g in range(2):
                        if n >= 2:
                            T.e.wait_ge(*stage(self.exped, 2 * (n - 1)))
                        for e in range(2):
                            head = 2 * g + e
                            for j in range(2):
                                mm = T.e.matmul(gp[:, g, e * SEQ:(e + 1) * SEQ], cols(4)[:, 2 * head + j, t * P:(t + 1) * P],
                                                cols(2)[:, 2 * head + j, :], start=j == 0, stop=j == 1)
                        mm.then_inc(*T.one(self.logit))
                        n += 1
                T.e.wait_ge(*stage(self.normed, NT))
                for head in range(X_HEADS):
                    if head >= 2:
                        T.e.wait_ge(*stage(self.p_columns, head - 1))
                    for c in range(2):
                        for t in range(NT):
                            mm = T.e.transpose(tp[:, head % 2, (2 * c + t) * P:(2 * c + t + 1) * P], self.probs[:, t, head, c * P:(c + 1) * P], ident)
                    mm.then_inc(*T.one(self.p_turned))
                for head in range(X_HEADS):
                    T.e.wait_ge(*stage(self.p_columns, head + 1))
                    if head >= 2:
                        T.e.wait_ge(*stage(self.o_done, head - 1))
                    for j in range(2):
                        for c in range(2):
                            mm = T.e.matmul(gp[:, head % 2, j * SEQ:(j + 1) * SEQ], rows(3)[:, c, head * XHD + j * P:head * XHD + (j + 1) * P],
                                            self.p_cols[:, c, head, :], start=c == 0, stop=c == 1)
                    mm.then_inc(*T.one(self.o))
                for b in range(2):
                    self.out.pe(T, b, XB, lambda t: acc[:, t, b * 512:(b + 1) * 512], (self.o_done, X_HEADS))

            def take_kv(self, A, b):
                split_hi(A, self.kv.last(b) + 4)
                A.e.wait_ge(chunk_used, self.kv.last(b))
                for t in range(NT):
                    A.e.activation(rows(1 if b < 2 else 3)[:, t, (b % 2) * 512:(b % 2 + 1) * 512], self.kv_bank(b)(t), ACT.Copy).then_inc(*A.one(self.kv_taken))

            def act(self, A):
                for b in range(4):
                    self.take_kv(A, b)
                self.k_turn.act_plain(A, cols(2), None)
                self.pre.act(A, h_rows, mix.post.done)
                for b in range(2):
                    split_hi(A, self.q.last(b) + 4)
                    A.e.wait_ge(chunk_used, self.q.last(b))
                    for t in range(NT):
                        A.e.activation(rows(6)[:, t, b * 512:(b + 1) * 512], acc[:, t, b * 512:(b + 1) * 512], ACT.Copy).then_inc(*A.one(self.q_taken))
                self.q_turn.act_plain(A, cols(4), None)
                n = 0
                for t in range(NT):
                    for g in range(2):
                        A.e.wait_ge(*stage(self.maxed, n + 1))
                        for e in range(2):
                            head = 2 * g + e
                            A.e.activation(self.probs[:, t, head, :], gp[:, g, e * SEQ:(e + 1) * SEQ], ACT.Exp, scale=XHD ** -0.5,
                                                bias=self.neg_max[:, 4 * t + head:4 * t + head + 1], accum_out=self.sums[:, 4 * t + head:4 * t + head + 1]).then_inc(*A.one(self.exped))
                        n += 1
                for head in range(X_HEADS):
                    A.e.wait_ge(*stage(self.p_turned, head + 1))
                    A.e.activation(self.p_cols[:, :, head, :], tp[:, head % 2, :].rearrange("p (c q) -> p c q", c=2), ACT.Copy).then_inc(*A.one(self.p_columns))
                for head in range(X_HEADS):
                    A.e.wait_ge(*stage(self.o, head + 1))
                    A.e.activation(XB[0][:, 2 * head:2 * head + 2, :].rearrange("p k s -> p (k s)"), gp[:, head % 2, :], ACT.Copy).then_inc(*A.one(self.o_hi))
                split_hi(A, self.out.end + 4)
                self.post.act(A, (chunk_used, self.out.end))

            def dve(self, V):
                split_lo(V, self.kv.end + 4)
                self.pre.dve(V, h_rows)
                split_lo(V, self.q.end + 4)
                n = 0
                for t in range(NT):
                    for g in range(2):
                        V.e.wait_ge(*stage(self.logit, n + 1))
                        m = self.neg_max[:, 4 * t + 2 * g:4 * t + 2 * g + 2]
                        V.e.tensor_reduce(m, gp[:, g, :].rearrange("p (h m) -> p h m", h=2), AX, ALU.max, negate=True).then_inc(*V.one())
                        V.e.wait_ge(*V.last)
                        V.e.tensor_scalar(m, m, XHD ** -0.5, None, ALU.mult).then_inc(*V.one(self.maxed))
                        n += 1
                for t in range(NT):
                    V.e.wait_ge(*stage(self.exped, 4 * (t + 1)))
                    s = self.sums[:, 4 * t:4 * t + 4]
                    V.e.reciprocal(s, s).then_inc(*V.one())
                    V.e.wait_ge(*V.last)
                    V.e.tensor_tensor(self.probs[:, t], self.probs[:, t], s.unsqueeze(2).to_broadcast([P, X_HEADS, SEQ]), ALU.mult).then_inc(*V.one(self.normed))
                for head in range(X_HEADS):
                    V.e.wait_ge(*stage(self.o_hi, head + 1))
                    hi = XB[0][:, 2 * head:2 * head + 2, :].rearrange("p k s -> p (k s)").bitcast(F32)
                    V.e.tensor_tensor(XB[1][:, 2 * head:2 * head + 2, :].rearrange("p k s -> p (k s)"), gp[:, head % 2, :], hi, ALU.subtract).then_inc(*V.one(self.o_done))
                split_lo(V, self.out.end + 4)
                self.post.dve(V)

        xattn = MemoryAttention()

        ffn2_pre = PreNorm(GAINS["ffn2_pre"], 6, XA)
        ffn2 = FeedForward(w["ffn2_w1"], w["ffn2_w3"], w["ffn2_w2"], DFF, XA, 5)
        ffn2_post = PostNorm(a["ffn2_post_g"][0], 0.5, 6, 1)

        class AddResidual:

            def __init__(self, name):
                self.done = sem(name + "_h")

            def dve(self, V, end):
                V.e.wait_ge(chunk_used, end)
                for t in range(NT):
                    V.e.tensor_tensor(h[:, t, :], acc[:, t, :], h[:, t, :], ALU.add).then_inc(*V.one(self.done))

        class TimeMix:
            R, K, V, W, A, G = range(6)
            GROUPS = R_HEADS // 4

            def __init__(self):
                n = "rwkv_"
                self.pre = PreNorm(GAINS["ln_mix"], 7, None)
                wr = a["a_w_rkv_2"][0]
                self.prods = [Product(wr[m], KT, [(0, 512), (512, 512)]) for m in range(3)]
                self.out = Product(a["a_wo_2"][0], KT, [(0, 512), (512, 512)])
                self.turn = ToColumns()
                self.add = AddResidual(n + "out")
                self.lora1_loaded, self.lora2_loaded, self.mixed, self.mixed_hi = sem(n + "lora1_loaded"), sem(n + "lora2_loaded"), sem(n + "mixed"), sem(n + "mixed_hi")
                self.mixed_lo, self.lora, self.low, self.w_up = sem(n + "mixed_lo"), sem(n + "lora"), sem(n + "low"), sem(n + "w_up")
                self.a_up, self.bias_loaded, self.w_in, self.w_sig = sem(n + "a_up"), sem(n + "bias_loaded"), sem(n + "w_in"), sem(n + "w_sig")
                self.log_w, self.a_in, self.a_ready, self.kk_raw = sem(n + "log_w"), sem(n + "a_in"), sem(n + "a_ready"), sem(n + "kk_raw")
                self.kk_ss, self.kk_rstd, self.b_rows, self.cum = sem(n + "kk_ss"), sem(n + "kk_rstd"), sem(n + "b_rows"), sem(n + "cum")
                self.decay, self.decay_ready, self.exp_c, self.exp_used = sem(n + "decay"), sem(n + "decay_ready"), sem(n + "exp_c"), sem(n + "exp_used")
                self.prev, self.prev_exp, self.rows_ready, self.turned = sem(n + "prev"), sem(n + "prev_exp"), sem(n + "rows_ready"), sem(n + "turned")
                self.cols, self.pairs, self.a_mat, self.first_inv = sem(n + "cols"), sem(n + "pairs"), sem(n + "a_mat"), sem(n + "first_inv")
                self.p, self.p_done, self.yx, self.yx_done = sem(n + "p"), sem(n + "p_done"), sem(n + "yx"), sem(n + "yx_done")
                self.rhs, self.rhs_done, self.u, self.u_done = sem(n + "rhs"), sem(n + "rhs_done"), sem(n + "u"), sem(n + "u_done")
                self.y, self.y_done, self.state_done = sem(n + "y"), sem(n + "y_done"), sem(n + "state_done")
                self.masked, self.identity = sem(n + "masked"), sem(n + "identity")
                self.g2_loaded, self.gate, self.centred, self.var = sem(n + "g2_loaded"), sem(n + "gate"), sem(n + "centred"), sem(n + "var")
                self.gn_rstd, self.bonus, self.y_rows, self.squared = sem(n + "gn_rstd"), sem(n + "bonus"), sem(n + "y_rows"), sem(n + "squared")
                self.taken = Later(mix.taken, 30)
                self.h_cols, self.xx, self.xs, self.xs_low = cols(0), cols(1), cols(7), cols(6)
                self.w1 = flat(2, 0, 512).rearrange("p (k n) -> p k n", k=KT)
                self.a1 = flat(2, 512, 512).rearrange("p (k n) -> p k n", k=KT)
                self.g1a = flat(2, 1024, 1024).rearrange("p (k n) -> p k n", k=KT)
                self.g1b = flat(3, 1792, 256).rearrange("p (k n) -> p k n", k=KT)
                self.up = flat(3, 0, 1024)
                self.low_cols = flat(3, 1024, 256)
                self.sig_g = flat(3, 1280, 512).rearrange("p (a s) -> p a s", a=2)
                self.tmp = flat(3, 0, 1024)
                self.ss, self.bonus_w, self.mean_s, self.var_s = stats(32), stats(32), stats(32), stats(32)
                self.decay_end = stats(8)
                spare = lambda first, n: raw[:, first:first + n].rearrange("p r j c -> p (r j c)")
                by_head = lambda x: x.rearrange("p (m s) -> p m s", m=4)
                places = (arena[1][:, :], spare(0, 2))
                self.fm = [[place[:, 1024 * s:1024 * (s + 1)].rearrange("p (j a s) -> p j a s", j=2, a=4) for s in range(2)] for place in places]
                self.mt = [place.rearrange("p (m a s) -> p m a s", m=4, a=4) for place in (arena[0][:, :], spare(2, 2))]
                self.x_inv = [by_head(flat(3, 0, 512)), by_head(spare(4, 1)[:, 0:512])]
                self.y_inv = [by_head(flat(3, 512, 512)), by_head(spare(4, 1)[:, 512:1024])]
                self.p_buf = [by_head(gain_b[0][:, 0:512]), by_head(spare(5, 1)[:, 0:512])]
                self.a_buf = [by_head(gain_b[0][:, 512:1024]), by_head(spare(5, 1)[:, 512:1024])]
                self.rhs_buf = [by_head(gain_b[1][:, 0:256]), by_head(flat(3, 1024, 256))]
                self.u_buf = [by_head(gain_b[1][:, 256:512]), by_head(flat(3, 1792, 256))]
                self.s_buf = gain_b[1][:, 512:1024].rearrange("p (c d) -> p c d", c=KT)

            def sp_lora(self, sp):
                sp.wait_ge(mix.o, 2 + X_HEADS)
                for dst, src in ((self.w1, a["a_w1_2"][0]), (self.a1, a["a_a1_2"][0])):
                    sp.dma_start(dst, src.rearrange("(k p) n -> p k n", p=P)).then_inc(self.lora1_loaded, 16)
                g1 = a["a_g1_2"][0].rearrange("(k p) n -> p k n", p=P)
                sp.dma_start(self.g1a, g1[:, :, 0:128]).then_inc(self.lora1_loaded, 16)
                sp.dma_start(self.g1b, g1[:, :, 128:160]).then_inc(self.lora1_loaded, 16)
                sp.dma_start(self.up[0:64, :], a["a_w2_2"][0]).then_inc(self.lora2_loaded, 16)
                sp.dma_start(self.up[64:128, :], a["a_a2_2"][0]).then_inc(self.lora2_loaded, 16)

            def sp(self, sp):
                ahead = self.ahead = self.out.first[0] + 4
                for c in range(self.prods[0].first[0], ahead):
                    load_chunk(sp, c)
                self.loads = 0
                for b, v, wait in ((0, a["a_w0_2"][0], xattn.post.freed), (1, a["a_a0_2"][0], ffn2_post.freed),
                                   (0, a["a_k_k_2"][0], (self.w_in, NT)), (1, a["a_k_a_2"][0], (self.a_in, NT)),
                                   (0, a["a_r_k_2"][0].rearrange("h d -> (h d)"), (self.kk_raw, NT))):
                    sp.wait_ge(*wait)
                    sp.dma_start(gain_b[b][:, :], v.partition_broadcast(P)).then_inc(self.bias_loaded, 16)
                    self.loads += 1
                    sp.wait_ge(self.bias_loaded, 16 * self.loads)
                sp.wait_ge(self.y_done, 2 * self.GROUPS - 2)
                sp.dma_start(flat(1, 0, 1024), a["a_g2_2"][0][0:128, :]).then_inc(self.g2_loaded, 16)
                sp.dma_start(flat(1, 1024, 1024)[0:32, :], a["a_g2_2"][0][128:160, :]).then_inc(self.g2_loaded, 16)
                sp.wait_ge(self.g2_loaded, 32)
                sp.wait_ge(self.y_done, 2 * self.GROUPS)
                for b, v in ((0, a["a_gn_g_2"][0]), (1, a["a_gn_b_2"][0])):
                    sp.dma_start(gain_b[b][:, :], v.partition_broadcast(P)).then_inc(self.g2_loaded, 16)
                for c in range(ahead, self.out.end):
                    load_chunk(sp, c)

            def pool(self, G):
                self.pre.pool(G)
                for t in range(NT):
                    G.e.wait_ge(self.kk_ss, t + 1)
                    s = self.ss[:, 16 * t:16 * t + 16]
                    G.e.tensor_tensor(s, s, half[:, 0:1].to_broadcast([P, 16]), ALU.pow).then_inc(*G.one(self.kk_rstd))
                for t in range(NT):
                    G.e.wait_ge(self.var, t + 1)
                    s = self.var_s[:, 16 * t:16 * t + 16]
                    G.e.tensor_tensor(s, s, half[:, 0:1].to_broadcast([P, 16]), ALU.pow).then_inc(*G.one(self.gn_rstd))

            def bank(self, q):
                return (lambda t: gp[:, t, :], lambda t: acc[:, t, 0:512], lambda t: acc[:, t, 512:1024])[q % 3]

            MIX = (R, W, K, A, G, V)

            def mu(self, n, k):
                at = GAINS["mu"] + 8 * n + k
                return gains[:, at:at + 1]

            def dve_mixed(self, V):
                self.pre.dve(V, h_rows, plain=True)
                V.e.wait_ge(*self.pre.turn.complete())
                V.e.tensor_tensor(self.xx[:, :, 1:SEQ], self.h_cols[:, :, 0:SEQ - 1], self.h_cols[:, :, 1:SEQ], ALU.subtract).then_inc(*V.one())
                V.e.tensor_scalar(self.xx[:, :, 0:1], self.h_cols[:, :, 0:1], -1.0, None, ALU.mult).then_inc(*V.one())
                V.e.wait_ge(*V.last)
                sets = {self.R: XA, self.K: XB, self.V: XA}
                made = {self.R: 0, self.K: 1, self.V: 2}
                count = 0
                for n in self.MIX:
                    big = n in sets
                    dst = self.xs if big else self.xs_low
                    if n == self.K:
                        V.e.wait_ge(self.mixed_lo, 1)
                    if n in (self.A, self.G):
                        V.e.wait_ge(self.lora, 1 if n == self.A else 2)
                    if n == self.V:
                        V.e.wait_ge(self.mixed_lo, 2)
                    for k in range(KT):
                        V.e.scalar_tensor_tensor(dst[:, k, :], self.xx[:, k, :], self.mu(n, k), self.h_cols[:, k, :], ALU.mult, ALU.add).then_inc(*V.one(self.mixed))
                    count += KT
                    if big:
                        x = sets[n]
                        V.e.wait_ge(self.mixed_hi, made[n] + 1)
                        V.e.wait_ge(*V.last)
                        V.e.tensor_tensor(x[1][:, :, :], dst, x[0][:, :, :].bitcast(F32), ALU.subtract).then_inc(*V.one(self.mixed_lo))
                    split_lo(V, self.prods[made.get(n, {self.W: 0, self.A: 1, self.G: 1}.get(n))].end + (1 if n == self.R else 0))

            def act_mixed(self, A):
                self.pre.act(A, h_rows, ffn2_post.done, plain=self.h_cols)
                sets = {self.R: XA, self.K: XB, self.V: XA}
                count = 0
                q = 0
                for n in self.MIX:
                    count += KT
                    if n in sets:
                        A.e.wait_ge(self.mixed, count)
                        if n == self.V:
                            A.e.wait_ge(chunk_used, self.prods[0].end)
                        A.e.activation(sets[n][0][:, :, :], self.xs, ACT.Copy).then_inc(*A.one(self.mixed_hi))
                        p = self.prods[{self.R: 0, self.K: 1, self.V: 2}[n]]
                        split_hi(A, p.end)
                        self.take(A, p, q, {self.R: 4, self.K: 5}.get(n)) if n != self.V else None
                        q += 2
                    elif n == self.W:
                        A.e.wait_ge(self.lora, 1)
                        A.e.activation(self.low_cols[0:64, :], tp[0:64, 0, 0:256], ACT.Tanh).then_inc(*A.one(self.low))
                    elif n == self.A:
                        A.e.wait_ge(self.lora, 2)
                        A.e.activation(self.low_cols[64:128, :], tp[64:128, 1, 0:256], ACT.Copy).then_inc(*A.one(self.low))
                    else:
                        A.e.wait_ge(self.lora, 3)
                        A.e.activation(self.sig_g[:, 0, :], tp[:, 0, 256:512], ACT.Sigmoid).then_inc(*A.one(self.low))
                        A.e.wait_ge(self.lora, 4)
                        A.e.activation(self.sig_g[0:32, 1, :], tp[0:32, 1, 256:512], ACT.Sigmoid).then_inc(*A.one(self.low))
                self.take(A, self.prods[2], 4, 6)

            def take(self, A, p, q, slot):
                for b in range(2):
                    split_hi(A, p.last(b) + 4)
                    A.e.wait_ge(chunk_used, p.last(b))
                    for t in range(NT):
                        A.e.activation(rows(slot)[:, t, b * 512:(b + 1) * 512], self.bank(q + b)(t), ACT.Copy).then_inc(*A.one(self.taken))

            def pe_product(self, T, m, x, made):
                for b in range(2):
                    q = 2 * m + b
                    self.prods[m].pe(T, b, x, self.bank(q), (self.mixed_lo, made), (self.taken, 2 * (q - 2)) if q >= 3 else None)

            def pe_lora(self, T, dst, weights, ready):
                T.e.wait_ge(self.mixed, ready)
                for k in range(KT):
                    mm = T.e.matmul(dst, weights[:, k, :], self.xs_low[:, k, :], start=k == 0, stop=k == KT - 1)
                mm.then_inc(*T.one(self.lora))

            def pe_mixed(self, T):
                self.pre.pe(T)
                self.pe_product(T, 0, XA, 1)
                T.e.wait_ge(self.lora1_loaded, 64)
                T.e.wait_ge(*self.pre.turn.complete())
                self.pe_lora(T, tp[0:64, 0, 0:256], self.w1, 2 * KT)
                self.pe_product(T, 1, XB, 2)
                self.pe_lora(T, tp[64:128, 1, 0:256], self.a1, 4 * KT)
                T.e.wait_ge(self.low, 2)
                self.pe_lora(T, tp[:, 0, 256:512], self.g1a, 5 * KT)
                self.pe_lora(T, tp[0:32, 1, 256:512], self.g1b, 5 * KT)
                self.pe_product(T, 2, XA, 3)

            def pe_rows(self, T):
                T.e.wait_ge(self.lora2_loaded, 32)
                T.e.wait_ge(self.low, 4)
                T.e.wait_ge(*stage(self.taken, 12))
                for e, done in ((0, self.w_up), (1, self.a_up)):
                    if e == 1:
                        T.e.wait_ge(self.w_in, NT)
                    for t in range(NT):
                        for b in range(2):
                            mm = T.e.matmul(acc[:, t, b * 512:(b + 1) * 512], self.low_cols[64 * e:64 * e + 64, t * P:(t + 1) * P],
                                            self.up[64 * e:64 * e + 64, b * 512:(b + 1) * 512], start=True, stop=True)
                        mm.then_inc(*T.one(done))
                T.e.wait_ge(self.a_in, NT)
                T.e.wait_ge(self.log_w, NT)
                for t in range(NT):
                    for b in range(2):
                        mm = T.e.matmul(acc[:, t, b * 512:(b + 1) * 512], const("tri"), rows(0)[:, t, b * 512:(b + 1) * 512], start=True, stop=True)
                    mm.then_inc(*T.one(self.cum))
                for c in range(KT):
                    for t in range(NT):
                        mm = T.e.matmul(tp[:, 1, c:c + 1], rows(0)[:, t, c * P:(c + 1) * P], const("ends")[:, t:t + 1], start=t == 0, stop=t == 1)
                mm.then_inc(*T.one(self.decay))

            def dve_rows(self, V):
                split_lo(V, self.prods[2].end + 4)
                hd = lambda x: x.rearrange("p (h d) -> p h d", d=HD)
                for e, (up, loaded, slot, done) in enumerate(((self.w_up, 16, 0, self.w_in), (self.a_up, 32, 1, self.a_in))):
                    V.e.wait_ge(self.bias_loaded, loaded)
                    for t in range(NT):
                        V.e.wait_ge(up, t + 1)
                        V.e.tensor_tensor(rows(slot)[:, t, :], acc[:, t, :], gain_b[e][:, :], ALU.add).then_inc(*V.one(done))
                V.e.wait_ge(self.w_sig, NT)
                for t in range(NT):
                    V.e.tensor_scalar(rows(0)[:, t, :], rows(0)[:, t, :], -DECAY, None, ALU.mult).then_inc(*V.one(self.log_w))
                V.e.wait_ge(self.bias_loaded, 48)
                V.e.wait_ge(*stage(self.taken, 12))
                for t in range(NT):
                    V.e.tensor_tensor(rows(7)[:, t, :], rows(5)[:, t, :], gain_b[0][:, :], ALU.mult).then_inc(*V.one(self.kk_raw))
                for t in range(NT):
                    s = self.ss[:, 16 * t:16 * t + 16]
                    V.e.wait_ge(*V.last)
                    V.e.tensor_tensor(self.tmp, rows(7)[:, t, :], rows(7)[:, t, :], ALU.mult).then_inc(*V.one())
                    V.e.wait_ge(*V.last)
                    V.e.tensor_reduce(s, hd(self.tmp), AX, ALU.add).then_inc(*V.one())
                    V.e.wait_ge(*V.last)
                    V.e.tensor_scalar(s, s, 1e-24, None, ALU.max).then_inc(*V.one(self.kk_ss))
                V.e.wait_ge(self.a_ready, NT)
                V.e.wait_ge(self.bias_loaded, 64)
                for t in range(NT):
                    V.e.wait_ge(*V.last)
                    V.e.scalar_tensor_tensor(self.tmp, rows(1)[:, t, :], -1.0, gain_b[1][:, :], ALU.add, ALU.mult).then_inc(*V.one())
                    V.e.wait_ge(*V.last)
                    V.e.scalar_tensor_tensor(rows(5)[:, t, :], self.tmp, 1.0, rows(5)[:, t, :], ALU.add, ALU.mult).then_inc(*V.one())
                for t in range(NT):
                    V.e.wait_ge(self.kk_rstd, t + 1)
                    s = self.ss[:, 16 * t:16 * t + 16].unsqueeze(2).to_broadcast([P, 16, HD])
                    V.e.tensor_tensor(hd(rows(7)[:, t, :]), hd(rows(7)[:, t, :]), s, ALU.mult).then_inc(*V.one())
                    V.e.wait_ge(*V.last)
                    V.e.tensor_tensor(rows(2)[:, t, :], rows(7)[:, t, :], rows(1)[:, t, :], ALU.mult).then_inc(*V.one(self.b_rows))
                V.e.wait_ge(self.bias_loaded, 80)
                for t in range(NT):
                    V.e.wait_ge(*V.last)
                    V.e.tensor_tensor(self.tmp, rows(4)[:, t, :], rows(5)[:, t, :], ALU.mult).then_inc(*V.one())
                    V.e.wait_ge(*V.last)
                    V.e.tensor_tensor(self.tmp, self.tmp, gain_b[0][:, :], ALU.mult).then_inc(*V.one())
                    V.e.wait_ge(*V.last)
                    V.e.tensor_reduce(self.bonus_w[:, 16 * t:16 * t + 16], hd(self.tmp), AX, ALU.add).then_inc(*V.one(self.bonus))
                for t in range(NT):
                    V.e.wait_ge(self.exp_c, 2 * t + 1)
                    V.e.tensor_tensor(rows(4)[:, t, :], rows(4)[:, t, :], rows(1)[:, t, :], ALU.mult).then_inc(*V.one(self.exp_used))
                    V.e.wait_ge(self.exp_c, 2 * t + 2)
                    V.e.wait_ge(*V.last)
                    V.e.tensor_tensor(rows(1)[:, t, :], acc[:, t, :], rows(0)[:, t, :], ALU.subtract).then_inc(*V.one(self.prev))
                    V.e.tensor_tensor(rows(5)[:, t, :], rows(5)[:, t, :], self.tmp, ALU.mult).then_inc(*V.one())
                    V.e.tensor_tensor(rows(2)[:, t, :], rows(2)[:, t, :], self.tmp, ALU.mult).then_inc(*V.one(self.exp_used))
                    V.e.wait_ge(self.prev_exp, t + 1)
                    V.e.scalar_tensor_tensor(rows(7)[:, t, :], rows(7)[:, t, :], -1.0, rows(1)[:, t, :], ALU.mult, ALU.mult).then_inc(*V.one(self.rows_ready))

            def act_rows(self, A):
                for slot, ready, done in ((0, self.w_in, self.w_sig), (1, self.a_in, self.a_ready)):
                    for t in range(NT):
                        A.e.wait_ge(ready, t + 1)
                        A.e.activation(rows(slot)[:, t, :], rows(slot)[:, t, :], ACT.Sigmoid).then_inc(*A.one(done))
                A.e.wait_ge(self.decay, 1)
                A.e.activation(self.decay_end, tp[:, 1, 0:KT], ACT.Exp).then_inc(*A.one(self.decay_ready))
                A.e.wait_ge(self.bonus, NT)
                for t in range(NT):
                    A.e.wait_ge(self.b_rows, t + 1)
                    if t == 1:
                        A.e.wait_ge(self.exp_used, 2)
                    A.e.activation(rows(1)[:, t, :], acc[:, t, :], ACT.Exp).then_inc(*A.one(self.exp_c))
                    A.e.activation(self.tmp, acc[:, t, :], ACT.Exp, scale=-1.0).then_inc(*A.one(self.exp_c))
                    A.e.wait_ge(self.prev, t + 1)
                    A.e.activation(rows(1)[:, t, :], rows(1)[:, t, :], ACT.Exp).then_inc(*A.one(self.prev_exp))

            def heads(self):
                return [(2 * e + j, e, j) for e in range(2) for j in range(2)]

            def stream_banks(self, s):
                return acc[:, s, 0:512], acc[:, s, 512:1024], gp[:, s, :], tp[:, s, :]

            def head_rows(self, slot, t, g, e, j):
                at = (4 * g + 2 * j + e) * HD
                return rows(slot)[:, t, at:at + HD]

            def pe_columns(self, T, p, s):
                t, g = divmod(2 * p + s, self.GROUPS)
                for j in range(2):
                    bank = self.stream_banks(s)[2 + j]
                    for n, slot in enumerate((7, 4, 2, 5)):
                        c0 = (2 * g + j) * P
                        mm = T.e.transpose(bank[:, n * P:(n + 1) * P], rows(slot)[:, t, c0:c0 + P], ident)
                    mm.then_inc(*T.one(self.turned))

            def pe_core(self, T):
                T.e.wait_ge(self.decay_ready, 1)
                T.e.wait_ge(self.rows_ready, NT)
                for s in range(2):
                    self.pe_columns(T, 0, s)
                for p in range(self.GROUPS):
                    t = 2 * p // self.GROUPS
                    for s in range(2):
                        fm = self.fm[p % 2][s]
                        T.e.wait_ge(self.cols, 4 * p + 2 * s + 2)
                        if p:
                            T.e.wait_ge(self.y_done, 2 * (p - 1) + s + 1)
                            T.e.wait_ge(self.state_done, min(2 * (p - 1) + s + 1, self.GROUPS))
                        for m, e, j in self.heads():
                            part = slice(e * HD, (e + 1) * HD)
                            ar = fm[part, j, 0:2, :].rearrange("p a s -> p (a s)")
                            T.e.matmul(self.stream_banks(s)[m][:, 0:256], fm[part, j, 2, :], ar, start=True, stop=True)
                            mm = T.e.matmul(self.stream_banks(s)[m][:, 256:512], fm[part, j, 3, :], ar, start=True, stop=True)
                            mm.then_inc(*T.one(self.pairs))
                    for s in range(2):
                        fm = self.fm[p % 2][s]
                        T.e.wait_ge(self.masked, 8 * p + 4 * s + 2)
                        for m, e, j in self.heads():
                            part = slice(e * HD, (e + 1) * HD)
                            mm = T.e.matmul(acc[:, s, e * 512 + j * P:e * 512 + (j + 1) * P], fm[part, j, 0, :], fm[part, j, 2, :], start=True, stop=True)
                        mm.then_inc(*T.one(self.a_mat))
                    for n in range(LEVELS):
                        for s in range(2):
                            if n == 0:
                                T.e.wait_ge(self.first_inv, 4 * p + 2 * s + 2)
                            else:
                                T.e.wait_ge(self.yx_done, self.yx_count(p, n - 1, s) + 1)
                            for m in range(4):
                                mm = T.e.matmul(gp[:, s, m * P:(m + 1) * P], self.a_buf[s][:, m, :], self.y_inv[s][:, m, :], start=True, stop=True)
                            mm.then_inc(*T.one(self.p))
                        for s in range(2):
                            if n:
                                T.e.wait_ge(self.yx_done, self.yx_count(p, n - 1, s) + 2)
                            T.e.wait_ge(self.p_done, 2 * (LEVELS * p + n) + s + 1)
                            for m in range(4):
                                mm = T.e.matmul(acc[:, s, m * P:(m + 1) * P], self.x_inv[s][:, m, :], self.p_buf[s][:, m, :], start=True, stop=True)
                            mm.then_inc(*T.one(self.yx))
                            if n < LEVELS - 1:
                                for m in range(4):
                                    mm = T.e.matmul(acc[:, s, 512 + m * P:512 + (m + 1) * P], self.p_buf[s][:, m, :], self.x_inv[s][:, m, :], start=True, stop=True)
                                mm.then_inc(*T.one(self.yx))
                    if t:
                        T.e.wait_ge(self.state_done, self.GROUPS)
                    for s in range(2):
                        g, fm = (2 * p + s) % self.GROUPS, self.fm[p % 2][s]
                        T.e.wait_ge(self.yx_done, self.yx_count(p, LEVELS - 1, s) + 1)
                        for m, e, j in self.heads():
                            dst = acc[:, s, e * 512 + j * HD:e * 512 + (j + 1) * HD]
                            mm = T.e.matmul(dst, self.mt[s][:, m, 2, :], self.head_rows(6, t, g, e, j), start=True, stop=t == 0)
                            if t:
                                part = slice(e * HD, (e + 1) * HD)
                                mm = T.e.matmul(dst, fm[part, j, 0, :], self.s_buf[part, 2 * g + j, :], start=False, stop=True)
                        mm.then_inc(*T.one(self.rhs))
                    if p < self.GROUPS - 1:
                        self.pe_columns(T, p + 1, 0)
                    for s in range(2):
                        T.e.wait_ge(self.rhs_done, 2 * p + s + 1)
                        for m in range(4):
                            mm = T.e.matmul(acc[:, s, m * HD:(m + 1) * HD], self.y_inv[s][:, m, :], self.rhs_buf[s][:, m, :], start=True, stop=True)
                        mm.then_inc(*T.one(self.u))
                    if p < self.GROUPS - 1:
                        self.pe_columns(T, p + 1, 1)
                    for s in range(2):
                        g, fm = (2 * p + s) % self.GROUPS, self.fm[p % 2][s]
                        T.e.wait_ge(self.u_done, 2 * p + s + 1)
                        for m, e, j in self.heads():
                            dst = acc[:, s, e * 512 + j * HD:e * 512 + (j + 1) * HD]
                            T.e.matmul(dst, self.mt[s][:, m, 1, :], self.u_buf[s][:, m, :], start=True, stop=False)
                            mm = T.e.matmul(dst, self.mt[s][:, m, 3, :], self.head_rows(6, t, g, e, j), start=False, stop=t == 0)
                            if t:
                                part = slice(e * HD, (e + 1) * HD)
                                mm = T.e.matmul(dst, fm[part, j, 1, :], self.s_buf[part, 2 * g + j, :], start=False, stop=True)
                        if t == 0:
                            for m, e, j in self.heads():
                                dst = acc[e * HD:(e + 1) * HD, s, 256 + j * HD:256 + (j + 1) * HD]
                                T.e.matmul(dst, self.head_rows(2, t, g, e, j), self.u_buf[s][:, m, :], start=True, stop=False)
                                mm = T.e.matmul(dst, self.head_rows(5, t, g, e, j), self.head_rows(6, t, g, e, j), start=False, stop=True)
                        mm.then_inc(*T.one(self.y))

            def yx_count(self, p, n, s):
                return 2 * p * (2 * LEVELS - 1) + 4 * n + (2 * s if n < LEVELS - 1 else s)

            def act_columns(self, A, p, s):
                for j in range(2):
                    A.e.wait_ge(self.turned, 4 * p + 2 * s + j + 1)
                    A.e.activation(self.fm[p % 2][s][:, j].rearrange("p a s -> p (a s)"), self.stream_banks(s)[2 + j], ACT.Copy).then_inc(*A.one(self.cols))

            def act_identity(self, A, s):
                for dst in (self.y_inv[s], self.x_inv[s]):
                    A.e.activation(dst, ident.unsqueeze(1).to_broadcast([P, 4, P]), ACT.Copy).then_inc(*A.one(self.identity))

            def act_core(self, A):
                A.e.wait_ge(self.rows_ready, NT)
                A.e.wait_ge(lo_done, self.out.first[0] + 4)
                for s in range(2):
                    self.act_identity(A, s)
                for s in range(2):
                    self.act_columns(A, 0, s)
                for p in range(self.GROUPS):
                    for n in range(LEVELS):
                        for s in range(2):
                            A.e.wait_ge(self.p, 2 * (LEVELS * p + n) + s + 1)
                            A.e.activation(self.p_buf[s].rearrange("p m s -> p (m s)"), gp[:, s, :], ACT.Copy).then_inc(*A.one(self.p_done))
                    if p < self.GROUPS - 1:
                        self.act_columns(A, p + 1, 0)
                    for s in range(2):
                        A.e.wait_ge(self.u, 2 * p + s + 1)
                        A.e.activation(self.u_buf[s].rearrange("p m d -> p (m d)"), acc[:, s, 0:256], ACT.Copy).then_inc(*A.one(self.u_done))
                    if p < self.GROUPS - 1:
                        self.act_columns(A, p + 1, 1)
                    for s in range(2):
                        t, g = divmod(2 * p + s, self.GROUPS)
                        A.e.wait_ge(self.y, 2 * p + s + 1)
                        dst = rows(7)[:, t, g * 256:(g + 1) * 256].rearrange("p (j e d) -> p e j d", j=2, e=2)
                        src = acc[:, s, :].rearrange("p (e x) -> p e x", e=2)[:, :, 0:128].rearrange("p e (j d) -> p e j d", j=2)
                        A.e.activation(dst, src, ACT.Copy).then_inc(*A.one(self.y_done))
                    if p < self.GROUPS - 1:
                        for s in range(2):
                            self.act_identity(A, s)

            def dve_core(self, V):
                four = lambda mask: mask.unsqueeze(1).to_broadcast([P, 4, P])
                low = const("lower").unsqueeze(1).to_broadcast([P, 2, P])
                for p in range(self.GROUPS):
                    for s in range(2):
                        for m in range(4):
                            V.e.wait_ge(self.pairs, 8 * p + 4 * s + m + 1)
                            V.e.tensor_tensor(self.mt[s][:, m].rearrange("p a s -> p (a s)"), self.stream_banks(s)[m], const("upper"), ALU.mult).then_inc(*V.one(self.masked))
                    for s in range(2):
                        V.e.wait_ge(self.identity, 4 * (p + 1))
                        V.e.wait_ge(self.masked, 8 * p + 4 * s + 4)
                        V.e.copy_predicated(self.y_inv[s], four(levels[:, 0, 0, :]), self.mt[s][:, :, 0, :]).then_inc(*V.one(self.first_inv))
                        V.e.wait_ge(self.a_mat, 2 * p + s + 1)
                        for e in range(2):
                            V.e.tensor_tensor(self.a_buf[s][:, 2 * e:2 * e + 2, :], acc[:, s, e * 512:e * 512 + 256].rearrange("p (j s) -> p j s", j=2), low, ALU.mult).then_inc(*V.one())
                        V.e.wait_ge(*V.last)
                        V.e.copy_predicated(self.x_inv[s], four(levels[:, 1, 0, :]), self.a_buf[s]).then_inc(*V.one(self.first_inv))
                    for n in range(LEVELS):
                        for s in range(2):
                            for x in range(2 if n < LEVELS - 1 else 1):
                                V.e.wait_ge(self.yx, self.yx_count(p, n, s) + x + 1)
                                dst = self.y_inv[s] if x == 0 else self.x_inv[s]
                                src = acc[:, s, x * 512:(x + 1) * 512].rearrange("p (m s) -> p m s", m=4)
                                V.e.copy_predicated(dst, four(levels[:, x, n + 1, :]), src).then_inc(*V.one(self.yx_done))
                    for s in range(2):
                        V.e.wait_ge(self.rhs, 2 * p + s + 1)
                        src = acc[:, s, :].rearrange("p (e x) -> p e x", e=2)[:, :, 0:128]
                        V.e.tensor_copy(self.rhs_buf[s].rearrange("p (e j) d -> p e (j d)", e=2), src).then_inc(*V.one(self.rhs_done))
                    for s in range(2):
                        t, g = divmod(2 * p + s, self.GROUPS)
                        if t == 0:
                            V.e.wait_ge(self.y_done, 2 * p + s + 1)
                            V.e.wait_ge(self.decay_ready, 1)
                            V.e.tensor_tensor(self.s_buf[:, 2 * g:2 * g + 2, :], acc[:, s, 256:384].rearrange("p (j d) -> p j d", j=2),
                                              self.decay_end[:, 2 * g:2 * g + 2].unsqueeze(2).to_broadcast([P, 2, HD]), ALU.mult).then_inc(*V.one(self.state_done))

            def pe_out(self, T):
                T.e.wait_ge(self.g2_loaded, 32)
                T.e.wait_ge(self.y_done, 2 * self.GROUPS)
                for t in range(NT):
                    for b in range(2):
                        dst = acc[:, t, b * 512:(b + 1) * 512]
                        T.e.matmul(dst, self.sig_g[:, 0, t * P:(t + 1) * P], flat(1, b * 512, 512), start=True, stop=False)
                        mm = T.e.matmul(dst, self.sig_g[0:32, 1, t * P:(t + 1) * P], flat(1, 1024 + b * 512, 512)[0:32, :], start=False, stop=True)
                    mm.then_inc(*T.one(self.gate))
                self.turn.pe(T, lambda k, t: rows(7)[:, t, k * P:(k + 1) * P], (self.y_rows, NT))
                for b in range(2):
                    self.out.pe(T, b, XA, lambda t: acc[:, t, b * 512:(b + 1) * 512], self.turn.complete())

            def act_out(self, A):
                for t in range(NT):
                    A.e.wait_ge(self.centred, t + 1)
                    A.e.activation(rows(4)[:, t, :], rows(7)[:, t, :], ACT.Square).then_inc(*A.one(self.squared))
                split_hi(A, self.out.first[0] + 5)
                self.turn.act(A, XA)
                split_hi(A, self.out.end + 4)

            def dve_out(self, V):
                V.e.wait_ge(self.y_done, 2 * self.GROUPS)
                hd = lambda x: x.rearrange("p (h d) -> p h d", d=HD)
                wide = lambda s: s.unsqueeze(2).to_broadcast([P, 16, HD])
                for t in range(NT):
                    y, mu_s = rows(7)[:, t, :], self.mean_s[:, 16 * t:16 * t + 16]
                    V.e.tensor_reduce(mu_s, hd(y), AX, ALU.add).then_inc(*V.one())
                    V.e.wait_ge(*V.last)
                    V.e.tensor_scalar(mu_s, mu_s, 1.0 / HD, None, ALU.mult).then_inc(*V.one())
                    V.e.wait_ge(*V.last)
                    V.e.tensor_tensor(hd(y), hd(y), wide(mu_s), ALU.subtract).then_inc(*V.one(self.centred))
                for t in range(NT):
                    v = hd(rows(6)[:, t, :])
                    V.e.tensor_tensor(v, v, wide(self.bonus_w[:, 16 * t:16 * t + 16]), ALU.mult).then_inc(*V.one())
                for t in range(NT):
                    V.e.wait_ge(self.squared, t + 1)
                    s = self.var_s[:, 16 * t:16 * t + 16]
                    V.e.tensor_reduce(s, hd(rows(4)[:, t, :]), AX, ALU.add).then_inc(*V.one())
                    V.e.wait_ge(*V.last)
                    V.e.tensor_scalar(s, s, 1.0 / HD, GN_EPS, ALU.mult, ALU.add).then_inc(*V.one(self.var))
                V.e.wait_ge(self.g2_loaded, 64)
                split_lo(V, self.out.first[0] + 5)
                for t in range(NT):
                    y = rows(7)[:, t, :]
                    V.e.wait_ge(self.gn_rstd, t + 1)
                    V.e.tensor_tensor(hd(y), hd(y), wide(self.var_s[:, 16 * t:16 * t + 16]), ALU.mult).then_inc(*V.one())
                    V.e.wait_ge(*V.last)
                    V.e.tensor_tensor(y, y, gain_b[0][:, :], ALU.mult).then_inc(*V.one())
                    V.e.wait_ge(*V.last)
                    V.e.tensor_tensor(y, y, gain_b[1][:, :], ALU.add).then_inc(*V.one())
                    V.e.wait_ge(*V.last)
                    V.e.tensor_tensor(y, y, rows(6)[:, t, :], ALU.add).then_inc(*V.one())
                    V.e.wait_ge(self.gate, t + 1)
                    V.e.wait_ge(*V.last)
                    V.e.tensor_tensor(y, y, acc[:, t, :], ALU.mult).then_inc(*V.one(self.y_rows))
                self.turn.dve(V, XA)
                split_lo(V, self.out.end + 4)
                self.add.dve(V, self.out.end)

        tmix = TimeMix()

        mlp1_pre = PreNorm(GAINS["ln_mlp"], 6, XA)
        mlp1 = FeedForward(a["mlp_w1_2"][0], None, a["mlp_w2_2"][0], MLP, XA, 5)
        mlp1_add = AddResidual("mlp1")

        class WindowAttention:
            HEADS, PER_KV = 16, 8
            KEYS, MASK_AT = Mix.KEYS, Mix.MASK_AT
            TOGETHER = tuple((4 * g + e, 4 * g + e + 2) for g in range(4) for e in range(2))

            def __init__(self):
                n = "window_"
                self.pre = PreNorm(GAINS["kv_norm"], 6, XB)
                self.q_in = ToColumns()
                self.kv = Product(a["w_kv_2"], KT, [(0, 256)])
                self.q = Product(a["b_wq_2"][0], KT, [(0, 512), (512, 512)])
                self.out = Product(a["b_wo_2"][0], KT, [(0, 512), (512, 512)])
                self.k_turn, self.q_turn = ToColumns(kts=2, plain=True), ToColumns(plain=True)
                self.add = AddResidual(n + "out")
                self.loaded, self.ss, self.rstd, self.k_rows = sem(n + "loaded"), sem(n + "ss"), sem(n + "rstd"), sem(n + "k_rows")
                self.q_rows, self.sink_in = sem(n + "q_rows"), sem(n + "sink_in")
                self.kv_taken, self.q_taken = Later(mix.taken, 42), Later(mix.taken, 44)
                self.logit, self.biased, self.maxed = Later(mix.logit, 12), Later(mix.biased, 16), Later(mix.maxed, 6)
                self.exped, self.normed = Later(mix.exped, 24), Later(mix.normed, 4)
                self.p_turned, self.p_cols = Later(mix.p_turned, 10), Later(mix.p_columns, 10)
                self.o, self.o_hi, self.o_done = Later(mix.o, 6), Later(mix.o_hi, 6), Later(mix.o_done, 6)
                self.sinks, self.k_gain, self.q_gain = stats(16), stats(64), stats(64)
                self.ss_k, self.ss_q = stats(4), stats(32)
                self.neg_max, self.sums, self.e_sink = stats(32), stats(32), stats(32)
                self.kv_rows = flat(0, 0, 512).rearrange("p (t n) -> p t n", t=NT)
                self.k_twice = flat(0, 512, 512).rearrange("p (t g c d) -> p t g c d", t=NT, g=2, c=2)
                self.k_cols = flat(1, 0, 512).rearrange("p (g s) -> p g s", g=2)
                self.squares = flat(0, 1024, 1024)
                wide = lambda slot, keys: arena[slot][:, :].rearrange("p (h s) -> p h s", s=keys)
                self.logits = [[wide(5, P)[:, 0:8], wide(5, P)[:, 8:16]], [wide(2, SEQ), wide(4, SEQ)]]
                self.p_col = {(0, 0): wide(6, P), (1, 0): wide(7, P), (1, 1): wide(3, P)}

            def logit_rows(self, t, head):
                return self.logits[t][head // 8][:, head % 8, :]

            def sp(self, sp):
                for dst, src in ((self.sinks, a["b_sinks_2"][0]), (self.k_gain, a["k_gain_2"]), (self.q_gain, a["b_q_gain_2"][0])):
                    sp.dma_start(dst, src.partition_broadcast(P)).then_inc(self.loaded, 16)
                for c in range(self.kv.first[0], self.out.end):
                    load_chunk(sp, c)

            def pool(self, G):
                self.pre.pool(G)
                for n, s in enumerate((self.ss_k, self.ss_q[:, 0:16], self.ss_q[:, 16:32])):
                    G.e.wait_ge(self.ss, n + 1)
                    G.e.tensor_tensor(s, s, half[:, 0:1].to_broadcast([P, s.shape[1]]), ALU.pow).then_inc(*G.one(self.rstd))

            def pbank(self, n):
                return (gp[:, 0, :], gp[:, 1, :], tp[:, 0, :], tp[:, 1, :])[n % 4]

            def obank(self, t, kv):
                return acc[:, t, kv * 512:(kv + 1) * 512]

            def pe(self, T):
                self.pre.pe(T)
                T.e.wait_ge(*self.pre.turn.complete())
                self.q_in.pe(T, lambda k, t: rows(6)[:, t, k * P:(k + 1) * P], (PreNorm.scaled, NT * (self.pre.n + 1)))
                self.kv.pe(T, 0, XB, lambda t: gp[:, t, :], self.pre.turn.complete())
                for b in range(2):
                    self.q.pe(T, b, XA, lambda t: acc[:, t, b * 512:(b + 1) * 512], self.q_in.complete())
                self.k_turn.pe(T, lambda k, t: self.k_twice[:, t, k].rearrange("p c d -> p (c d)"), (self.k_rows, NT))
                T.e.wait_ge(*self.k_turn.complete())
                self.q_turn.pe(T, lambda k, t: rows(2)[:, t, k * P:(k + 1) * P], (self.q_rows, NT))
                T.e.wait_ge(*self.q_turn.complete())
                n = 0
                for t in range(NT):
                    keys = self.KEYS[t]
                    for heads in self.TOGETHER:
                        if n >= 4:
                            T.e.wait_ge(*stage(self.biased, 2 * (n - 3)))
                        for j, head in enumerate(heads):
                            part = slice((head % 2) * HD, (head % 2 + 1) * HD)
                            mm = T.e.matmul(self.pbank(n)[:, j * keys:(j + 1) * keys], cols(3)[part, head // 2, t * P:(t + 1) * P],
                                            self.k_cols[part, head // self.PER_KV, 0:keys], start=True, stop=True)
                        mm.then_inc(*T.one(self.logit))
                        n += 1
                n = 0
                for t in range(NT):
                    T.e.wait_ge(*stage(self.normed, 2 * (t + 1)))
                    for c in range(t + 1):
                        for g in range(4):
                            if n >= 2:
                                T.e.wait_ge(*stage(self.p_cols, n - 1))
                            for j in range(4):
                                mm = T.e.transpose(tp[:, n % 2, j * P:(j + 1) * P], self.logit_rows(t, 4 * g + j)[:, c * P:(c + 1) * P], ident)
                            mm.then_inc(*T.one(self.p_turned))
                            n += 1
                for t in range(NT):
                    T.e.wait_ge(*stage(self.p_cols, 4 if t == 0 else 12))
                    for kv in range(2):
                        for e in range(2):
                            dst = self.obank(t, kv)[e * HD:(e + 1) * HD, :].rearrange("p (h q) -> p h q", h=4)
                            for c in range(t + 1):
                                mm = T.e.matmul(dst, self.kv_rows[:, c, P + kv * HD:P + (kv + 1) * HD],
                                                self.p_col[t, c][:, kv * 8 + e:kv * 8 + 8:2, :], start=c == 0, stop=c == t)
                        mm.then_inc(*T.one(self.o))
                for b in range(2):
                    self.out.pe(T, b, XB, lambda t: acc[:, t, b * 512:(b + 1) * 512], (self.o_done, 4))

            def act(self, A):
                self.pre.act(A, h_rows, (mlp1_add.done, NT))
                self.q_in.act(A, XA, GAINS["ln_mix"] + 8)
                split_hi(A, self.kv.end + 4)
                A.e.wait_ge(chunk_used, self.kv.end)
                for t in range(NT):
                    A.e.activation(self.kv_rows[:, t, :], gp[:, t, 0:256], ACT.Copy).then_inc(*A.one(self.kv_taken))
                for b in range(2):
                    split_hi(A, self.q.last(b) + 4)
                    A.e.wait_ge(chunk_used, self.q.last(b))
                    for t in range(NT):
                        A.e.activation(rows(2)[:, t, b * 512:(b + 1) * 512], acc[:, t, b * 512:(b + 1) * 512], ACT.Copy).then_inc(*A.one(self.q_taken))
                self.k_turn.act_plain(A, self.k_cols, None)
                self.q_turn.act_plain(A, cols(3), None)
                for t in range(NT):
                    A.e.wait_ge(*stage(self.maxed, t + 1))
                    for head in range(self.HEADS):
                        at = 16 * t + head
                        lg = self.logit_rows(t, head)
                        A.e.activation(lg, lg, ACT.Exp, bias=self.neg_max[:, at:at + 1], accum_out=self.sums[:, at:at + 1]).then_inc(*A.one(self.exped))
                    s = self.e_sink[:, 16 * t:16 * t + 16]
                    A.e.wait_ge(self.sink_in, t + 1)
                    A.e.activation(s, s, ACT.Exp).then_inc(*A.one(self.exped))
                n = 0
                for t in range(NT):
                    for c in range(t + 1):
                        for g in range(4):
                            A.e.wait_ge(*stage(self.p_turned, n + 1))
                            A.e.activation(self.p_col[t, c][:, 4 * g:4 * g + 4, :].rearrange("p h q -> p (h q)"), tp[:, n % 2, :], ACT.Copy).then_inc(*A.one(self.p_cols))
                            n += 1
                n = 0
                for t in range(NT):
                    for kv in range(2):
                        A.e.wait_ge(*stage(self.o, n + 1))
                        A.e.activation(XB[0][:, 4 * kv:4 * kv + 4, t * P:(t + 1) * P], self.obank(t, kv).rearrange("p (h q) -> p h q", h=4), ACT.Copy).then_inc(*A.one(self.o_hi))
                        n += 1
                split_hi(A, self.out.end + 4)

            def dve(self, V):
                hd = lambda x: x.rearrange("p (h d) -> p h d", d=HD)
                self.pre.dve(V, h_rows)
                self.q_in.dve(V, XA, GAINS["ln_mix"] + 8)
                split_lo(V, self.kv.end + 4)
                V.e.wait_ge(self.loaded, 48)
                V.e.tensor_scalar(self.q_gain, self.q_gain, HD ** -0.5, None, ALU.mult).then_inc(*V.one())
                V.e.wait_ge(*stage(self.kv_taken, NT))
                sq = self.squares[:, 0:256].rearrange("p (t n) -> p t n", t=NT)
                V.e.tensor_tensor(sq, self.kv_rows[:, :, 0:P], self.kv_rows[:, :, 0:P], ALU.mult).then_inc(*V.one())
                V.e.wait_ge(*V.last)
                V.e.tensor_reduce(self.ss_k, hd(self.squares[:, 0:256]), AX, ALU.add).then_inc(*V.one())
                V.e.wait_ge(*V.last)
                V.e.tensor_scalar(self.ss_k, self.ss_k, 1.0 / HD, EPS, ALU.mult, ALU.add).then_inc(*V.one(self.ss))
                V.e.wait_ge(self.rstd, 1)
                for t in range(NT):
                    k = hd(self.kv_rows[:, t, 0:P])
                    V.e.wait_ge(*V.last)
                    V.e.tensor_tensor(k, k, self.ss_k[:, 2 * t:2 * t + 2].unsqueeze(2).to_broadcast([P, 2, HD]), ALU.mult).then_inc(*V.one())
                    V.e.wait_ge(*V.last)
                    for c in range(2):
                        V.e.tensor_tensor(self.k_twice[:, t, :, c, :], k, self.k_gain.unsqueeze(1).to_broadcast([P, 2, HD]), ALU.mult).then_inc(*V.one(self.k_rows if c else None))
                split_lo(V, self.q.end + 4)
                V.e.wait_ge(*stage(self.q_taken, 4))
                for t in range(NT):
                    q, s = rows(2)[:, t, :], self.ss_q[:, 16 * t:16 * t + 16]
                    V.e.wait_ge(*V.last)
                    V.e.tensor_tensor(self.squares, q, q, ALU.mult).then_inc(*V.one())
                    V.e.wait_ge(*V.last)
                    V.e.tensor_reduce(s, hd(self.squares), AX, ALU.add).then_inc(*V.one())
                    V.e.wait_ge(*V.last)
                    V.e.tensor_scalar(s, s, 1.0 / HD, EPS, ALU.mult, ALU.add).then_inc(*V.one(self.ss))
                for t in range(NT):
                    q = hd(rows(2)[:, t, :])
                    V.e.wait_ge(self.rstd, t + 2)
                    V.e.wait_ge(*V.last)
                    V.e.tensor_tensor(q, q, self.ss_q[:, 16 * t:16 * t + 16].unsqueeze(2).to_broadcast([P, 16, HD]), ALU.mult).then_inc(*V.one())
                    V.e.wait_ge(*V.last)
                    V.e.tensor_tensor(q, q, self.q_gain.unsqueeze(1).to_broadcast([P, 16, HD]), ALU.mult).then_inc(*V.one(self.q_rows))
                V.e.wait_ge(*self.q_turn.complete())
                n = 0
                for t in range(NT):
                    keys = self.KEYS[t]
                    for heads in self.TOGETHER:
                        V.e.wait_ge(*stage(self.logit, n + 1))
                        for j, head in enumerate(heads):
                            slope = 2.0 ** (-8.0 * (head + 1) / self.HEADS)
                            V.e.scalar_tensor_tensor(self.logit_rows(t, head), const("dist")[:, self.MASK_AT[t]:self.MASK_AT[t] + keys], -slope,
                                                          self.pbank(n)[:, j * keys:(j + 1) * keys], ALU.mult, ALU.add).then_inc(*V.one(self.biased))
                        n += 1
                for t in range(NT):
                    m = self.neg_max[:, 16 * t:16 * t + 16]
                    V.e.wait_ge(*V.last)
                    for g in range(2):
                        V.e.tensor_reduce(m[:, 8 * g:8 * g + 8], self.logits[t][g], AX, ALU.max).then_inc(*V.one())
                    V.e.wait_ge(*V.last)
                    V.e.tensor_tensor(m, m, self.sinks, ALU.max).then_inc(*V.one())
                    V.e.wait_ge(*V.last)
                    V.e.tensor_scalar(m, m, -1.0, None, ALU.mult).then_inc(*V.one(self.maxed))
                    V.e.wait_ge(*V.last)
                    V.e.tensor_tensor(self.e_sink[:, 16 * t:16 * t + 16], self.sinks, m, ALU.add).then_inc(*V.one(self.sink_in))
                for t in range(NT):
                    V.e.wait_ge(*stage(self.exped, 17 * (t + 1)))
                    s = self.sums[:, 16 * t:16 * t + 16]
                    V.e.tensor_tensor(s, s, self.e_sink[:, 16 * t:16 * t + 16], ALU.add).then_inc(*V.one())
                    V.e.wait_ge(*V.last)
                    V.e.reciprocal(s, s).then_inc(*V.one())
                    V.e.wait_ge(*V.last)
                    for g in range(2):
                        x = self.logits[t][g]
                        V.e.tensor_tensor(x, x, s[:, 8 * g:8 * g + 8].unsqueeze(2).to_broadcast([P, 8, self.KEYS[t]]), ALU.mult).then_inc(*V.one(self.normed))
                n = 0
                for t in range(NT):
                    for kv in range(2):
                        V.e.wait_ge(*stage(self.o_hi, n + 1))
                        at = (slice(None), slice(4 * kv, 4 * kv + 4), slice(t * P, (t + 1) * P))
                        V.e.tensor_tensor(XB[1][at], self.obank(t, kv).rearrange("p (h q) -> p h q", h=4), XB[0][at].bitcast(F32), ALU.subtract).then_inc(*V.one(self.o_done))
                        n += 1
                split_lo(V, self.out.end + 4)
                self.add.dve(V, self.out.end)

        window = WindowAttention()

        mlp2_pre = PreNorm(GAINS["ln_mlp"] + 8, 6, XA)
        mlp2 = FeedForward(a["mlp_w1_2"][1], None, a["mlp_w2_2"][1], MLP, XA, 5)
        mlp2_add = AddResidual("mlp2")

        pres = [ffn1_pre, mix.pre, xattn.mem_pre, xattn.pre, ffn2_pre, tmix.pre, mlp1_pre, window.pre, mlp2_pre]
        posts = [ffn1_post, mix.post, xattn.post, ffn2_post]
        norms = [ffn1_pre, ffn1_post, mix.pre, xattn.mem_pre, mix.post, xattn.pre, xattn.post, ffn2_pre, ffn2_post, tmix.pre,
                 mlp1_pre, window.pre, mlp2_pre]
        turns = [ffn1_pre.turn, mix.pre.turn, mix.merge, xattn.mem_pre.turn, xattn.k_turn, xattn.pre.turn, xattn.q_turn,
                 ffn2_pre.turn, tmix.pre.turn, tmix.turn, mlp1_pre.turn, window.pre.turn, window.q_in, window.k_turn,
                 window.q_turn, mlp2_pre.turn]
        layers = [ffn1, ffn2, mlp1, mlp2]
        for n, x in enumerate(pres):
            x.start(n)
        for n, x in enumerate(posts):
            x.start(n)
        for n, x in enumerate(norms):
            x.rms.start(n)
        for n, x in enumerate(turns):
            x.start(turns[:n])
        for n, x in enumerate(layers):
            x.start_counts(layers[:n])

        block = ctx.enter_context(nc.Block())

        @block.sync
        def _(sp):
            setup.sp(sp)
            ffn1_post.sp(sp)
            ffn1.sp(sp)
            mix.sp(sp)
            xattn.sp(sp)
            ffn2_post.sp(sp, mix.post.freed)
            tmix.sp_lora(sp)
            ffn2.sp(sp)
            tmix.sp(sp)
            mlp1.sp(sp)
            window.sp(sp)
            mlp2.sp(sp)
            sp.wait_ge(mlp2_add.done, NT)
            sp.dma_start(out[0].rearrange("(t p) d -> p t d", p=P), h[:, :, :]).then_inc(out_stored, 16)
            sp.wait_ge(out_stored, 16)

        @block.gpsimd
        def _(pool):
            G = Lane(pool, pool_results)
            setup.pool(G)
            ffn1_pre.pool(G)
            ffn1_post.pool(G)
            mix.pool(G)
            xattn.mem_pre.pool(G)
            mix.post.pool(G)
            xattn.pre.pool(G)
            xattn.post.pool(G)
            ffn2_pre.pool(G)
            ffn2_post.pool(G)
            tmix.pool(G)
            mlp1_pre.pool(G)
            window.pool(G)
            mlp2_pre.pool(G)

        @block.scalar
        def _(act):
            A = Lane(act, act_results)
            setup.act(A)
            ffn1_pre.act(A, h_rows, (x_loaded, 32))
            ffn1.act(A)
            split_hi(A, ffn1.end + 5)
            ffn1_post.act(A, (chunk_used, ffn1.end))
            mix.act(A)
            xattn.act(A)
            ffn2_pre.act(A, h_rows, xattn.post.done)
            ffn2.act(A)
            split_hi(A, ffn2.end + 5)
            ffn2_post.act(A, (chunk_used, ffn2.end))
            tmix.act_mixed(A)
            tmix.act_rows(A)
            tmix.act_core(A)
            tmix.act_out(A)
            mlp1_pre.act(A, h_rows, (tmix.add.done, NT))
            mlp1.act(A)
            split_hi(A, mlp1.end + 3)
            window.act(A)
            mlp2_pre.act(A, h_rows, (window.add.done, NT))
            mlp2.act(A)
            split_hi(A, mlp2.end)

        @block.vector
        def _(dve):
            V = Lane(dve, dve_results)
            setup.dve(V)
            ffn1_pre.dve(V, h_rows)
            setup.dve_levels(V)
            ffn1.dve(V)
            split_lo(V, ffn1.end + 5)
            ffn1_post.dve(V)
            mix.dve(V)
            xattn.dve(V)
            ffn2_pre.dve(V, h_rows)
            ffn2.dve(V)
            split_lo(V, ffn2.end + 5)
            ffn2_post.dve(V)
            tmix.dve_mixed(V)
            tmix.dve_rows(V)
            tmix.dve_core(V)
            tmix.dve_out(V)
            mlp1_pre.dve(V, h_rows)
            mlp1.dve(V)
            split_lo(V, mlp1.end + 3)
            mlp1_add.dve(V, mlp1.end)
            window.dve(V)
            mlp2_pre.dve(V, h_rows)
            mlp2.dve(V)
            split_lo(V, mlp2.end)
            mlp2_add.dve(V, mlp2.end)

        @block.tensor
        def _(pe):
            T = Lane(pe, pe_results)
            setup.pe(T)
            ffn1_pre.pe(T)
            ffn1.pe(T, ffn1_pre.turn.complete())
            mix.pe(T)
            xattn.pe_memory(T)
            xattn.pe(T)
            ffn2_pre.pe(T)
            ffn2.pe(T, ffn2_pre.turn.complete(), xattn.post.freed)
            tmix.pe_mixed(T)
            tmix.pe_rows(T)
            tmix.pe_core(T)
            tmix.pe_out(T)
            mlp1_pre.pe(T)
            mlp1.pe(T, mlp1_pre.turn.complete(), (tmix.add.done, NT))
            window.pe(T)
            mlp2_pre.pe(T)
            mlp2.pe(T, mlp2_pre.turn.complete(), (window.add.done, NT))


_INS = ["x", "mem", "ffn1_pre_g", "ffn1_post_g", "ffn1_w1", "ffn1_w3", "ffn1_w2", "mix_pre_g", "mix_post_g", "w_in",
        "conv_w", "w_a_out", "w_b_out", "w_out", "mem_g", "xattn_pre_g", "xattn_post_g", "xattn_w_q", "xattn_w_kv",
        "xattn_w_o", "ffn2_pre_g", "ffn2_post_g", "ffn2_w1", "ffn2_w3", "ffn2_w2", "ln_mix_2", "ln_mlp_2", "mlp_w1_2",
        "mlp_w2_2", "a_mu_2", "a_w_rkv_2", "a_w0_2", "a_w1_2", "a_w2_2", "a_a0_2", "a_a1_2", "a_a2_2", "a_g1_2",
        "a_g2_2", "a_k_k_2", "a_k_a_2", "a_r_k_2", "a_gn_g_2", "a_gn_b_2", "a_wo_2", "kv_norm_2", "w_kv_2", "k_gain_2",
        "b_wq_2", "b_q_gain_2", "b_sinks_2", "b_wo_2"]


def kernel(**inputs):
    import concourse.bacc as bacc
    from concourse.bass_utils import run_bass_kernel_spmd

    nc = bacc.Bacc("TRN2", target_bir_lowering=False, num_devices=1)
    consts, levels = shape_constants()
    arrays = {n: np.ascontiguousarray(inputs[n]) for n in _INS}
    arrays["consts"], arrays["levels"] = consts, levels
    aps = {n: nc.dram_tensor(f"in_{n}", v.shape, mybir.dt.from_np(v.dtype), kind="ExternalInput").ap() for n, v in arrays.items()}
    out = nc.dram_tensor("out_0", (1, SEQ, D), F32, kind="ExternalOutput").ap()
    build(nc, aps, out)
    r = run_bass_kernel_spmd(nc, [{f"in_{n}": v for n, v in arrays.items()}], core_ids=[0])
    return r.results[0]["out_0"]
```
